# Optimizing a Trainium2 kernel written in Bass

```python
import math
import jax, jax.numpy as jnp
from jax import lax
import numpy as np

D_MODEL = 2048
BATCH = 1
SEQ = 256
DEPTH = 2

CHUNK = 64
N_MIXERS = 2
N_FOX = (DEPTH + 1) // 2
N_RWKV = DEPTH // 2

FOX_HEADS = 16
FOX_HEAD_DIM = D_MODEL // FOX_HEADS
Q_BLOCK = 128

RWKV_HEAD_DIM = 64
RWKV_HEADS = D_MODEL // RWKV_HEAD_DIM
DECAY_LORA = 96
AAA_LORA = 96
GATE_LORA = 256

D_FF = 5632
CONV_WIDTH = 3
NORM_EPS = 1e-6
GN_EPS = 64e-5

kernel_name = "hybrid_fox_rwkv7_convffn_adaln"

def rms_norm(x, g):
    xf = x.astype(jnp.float32)
    y = xf * lax.rsqrt(jnp.mean(xf * xf, axis=-1, keepdims=True) + NORM_EPS)
    return (y * g.astype(jnp.float32)).astype(x.dtype)

def token_shift(x):
    return jnp.pad(x, ((0, 0), (1, 0), (0, 0)))[:, :-1]

def fox_attention(h, w_in, b_f, w_out):
    B, S, D = h.shape
    H, hd = FOX_HEADS, FOX_HEAD_DIM
    proj = h @ w_in
    q, k, v, f_logit = jnp.split(proj, [D, 2 * D, 3 * D], axis=-1)
    q = q.reshape(B, S, H, hd).transpose(0, 2, 1, 3)
    k = k.reshape(B, S, H, hd).transpose(0, 2, 1, 3)
    v = v.reshape(B, S, H, hd).transpose(0, 2, 1, 3)
    log_f = jax.nn.log_sigmoid((f_logit + b_f).astype(jnp.float32)).transpose(0, 2, 1)
    cum = jnp.cumsum(log_f, axis=-1)
    nb = S // Q_BLOCK
    qb = q.reshape(B, H, nb, Q_BLOCK, hd).transpose(2, 0, 1, 3, 4)
    cb = cum.reshape(B, H, nb, Q_BLOCK).transpose(2, 0, 1, 3)
    kpos = jnp.arange(S)
    scale = hd ** -0.5

    def block(args):
        i, q_i, c_i = args
        qpos = i * Q_BLOCK + jnp.arange(Q_BLOCK)
        logits = (jnp.einsum('bhqd,bhkd->bhqk', q_i, k).astype(jnp.float32) * scale
                  + c_i[..., :, None] - cum[..., None, :])
        logits = jnp.where(kpos[None, :] <= qpos[:, None], logits, -jnp.inf)
        p = jax.nn.softmax(logits, axis=-1)
        return jnp.einsum('bhqk,bhkd->bhqd', p.astype(v.dtype), v)

    ob = lax.map(block, (jnp.arange(nb), qb, cb))
    o = ob.transpose(1, 0, 3, 2, 4).reshape(B, S, D)
    return o @ w_out

def wkv7_scan(r, w, k, v, kk, a):
    B, S, H, N = r.shape
    nc = S // CHUNK

    def to_chunks(t):
        return t.reshape(B, nc, CHUNK, H, N).transpose(1, 2, 0, 3, 4)

    def step(state, inp):
        r_t, w_t, k_t, v_t, kk_t, a_t = inp
        sa = jnp.einsum('bhvk,bhk->bhv', state, kk_t)
        state = (state * w_t[:, :, None, :]
                 - sa[..., None] * (kk_t * a_t)[:, :, None, :]
                 + v_t[..., None] * k_t[:, :, None, :])
        y = jnp.einsum('bhvk,bhk->bhv', state, r_t)
        return state, y

    def chunk_step(state, inp):
        return lax.scan(step, state, inp)

    s0 = jnp.zeros((B, H, N, N), jnp.float32)
    xs = (to_chunks(r), to_chunks(w), to_chunks(k), to_chunks(v), to_chunks(kk), to_chunks(a))
    _, y = lax.scan(chunk_step, s0, xs)
    return y.transpose(2, 0, 1, 3, 4).reshape(B, S, H, N)

def rwkv7_time_mix(h, mu, w0, w1, w2, a0, a1, a2, g1, g2, k_k, k_a, r_k,
                   w_r, w_k, w_v, w_o, gn_w, gn_b):
    B, S, D = h.shape
    H, N = RWKV_HEADS, RWKV_HEAD_DIM
    xx = token_shift(h) - h
    mixed = h[None] + xx[None] * mu[:, None, None, :]
    xr, xw, xk, xv, xa, xg = mixed[0], mixed[1], mixed[2], mixed[3], mixed[4], mixed[5]
    r = xr @ w_r
    w_log = -jax.nn.softplus(-(w0 + jnp.tanh(xw @ w1) @ w2)) - 0.5
    decay = jnp.exp(-jnp.exp(w_log.astype(jnp.float32)))
    k = xk @ w_k
    v = xv @ w_v
    a = jax.nn.sigmoid(a0 + (xa @ a1) @ a2)
    g = jax.nn.sigmoid(xg @ g1) @ g2
    kk = k * k_k
    k = k * (1 + (a - 1) * k_a)

    def heads(t):
        return t.reshape(B, S, H, N).astype(jnp.float32)

    r_h, w_h, k_h, v_h, a_h = heads(r), heads(decay), heads(k), heads(v), heads(a)
    kk_h = heads(kk)
    kk_h = kk_h / jnp.maximum(jnp.sqrt(jnp.sum(kk_h * kk_h, axis=-1, keepdims=True)), 1e-12)
    y = wkv7_scan(r_h, w_h, k_h, v_h, kk_h, a_h)
    mean = jnp.mean(y, axis=-1, keepdims=True)
    var = jnp.mean(jnp.square(y - mean), axis=-1, keepdims=True)
    y = ((y - mean) * lax.rsqrt(var + GN_EPS)).reshape(B, S, D)
    y = y * gn_w.astype(jnp.float32) + gn_b.astype(jnp.float32)
    bonus = (jnp.sum(r_h * k_h * r_k.astype(jnp.float32), axis=-1, keepdims=True) * v_h).reshape(B, S, D)
    out = ((y + bonus).astype(h.dtype) * g)
    return out @ w_o

def conv_ffn(h, w_in, conv_w, conv_b, w_out):
    u = h @ w_in
    C = u.shape[-1]
    u = lax.conv_general_dilated(
        u, conv_w[:, None, :], window_strides=(1,), padding=[(CONV_WIDTH - 1, 0)],
        dimension_numbers=('NWC', 'WIO', 'NWC'), feature_group_count=C) + conv_b
    x1, x2 = jnp.split(u, 2, axis=-1)
    return (jax.nn.gelu(x1, approximate=False) * x2) @ w_out

def setup_inputs(seed: int = 0) -> dict:
    key = jax.random.key(seed)
    ks = jax.random.split(key, 32)
    D, F, H, N = D_MODEL, D_FF, FOX_HEADS, RWKV_HEAD_DIM
    nrm = lambda k, shape, s: jax.random.normal(k, shape, jnp.float32) * s
    return {
        "x": nrm(ks[0], (BATCH, SEQ, D), 1.0),
        "c": nrm(ks[1], (BATCH, D), 1.0),
        "mod_w": nrm(ks[2], (DEPTH, D, 6 * D), 0.5 * D ** -0.5),
        "mod_b": nrm(ks[3], (DEPTH, 6 * D), 0.01),
        "norm_g": 1.0 + nrm(ks[4], (DEPTH, 4, D), 0.05),
        "fox_w_in": nrm(ks[5], (N_FOX, D, 3 * D + H), D ** -0.5),
        "fox_b_f": jax.random.uniform(ks[6], (N_FOX, H), jnp.float32, 1.0, 5.0),
        "fox_w_out": nrm(ks[7], (N_FOX, D, D), D ** -0.5),
        "rwkv_mu": jax.random.uniform(ks[8], (N_RWKV, 6, D), jnp.float32),
        "rwkv_w0": jax.random.uniform(ks[9], (N_RWKV, D), jnp.float32, -6.0, -1.0),
        "rwkv_w1": nrm(ks[10], (N_RWKV, D, DECAY_LORA), D ** -0.5),
        "rwkv_w2": nrm(ks[11], (N_RWKV, DECAY_LORA, D), 0.1 * DECAY_LORA ** -0.5),
        "rwkv_a0": nrm(ks[12], (N_RWKV, D), 0.1),
        "rwkv_a1": nrm(ks[13], (N_RWKV, D, AAA_LORA), D ** -0.5),
        "rwkv_a2": nrm(ks[14], (N_RWKV, AAA_LORA, D), 0.1 * AAA_LORA ** -0.5),
        "rwkv_g1": nrm(ks[15], (N_RWKV, D, GATE_LORA), D ** -0.5),
        "rwkv_g2": nrm(ks[16], (N_RWKV, GATE_LORA, D), GATE_LORA ** -0.5),
        "rwkv_k_k": 0.85 + nrm(ks[17], (N_RWKV, D), 0.05),
        "rwkv_k_a": 1.0 + nrm(ks[18], (N_RWKV, D), 0.05),
        "rwkv_r_k": nrm(ks[19], (N_RWKV, RWKV_HEADS, N), 0.1),
        "rwkv_w_r": nrm(ks[20], (N_RWKV, D, D), D ** -0.5),
        "rwkv_w_k": nrm(ks[21], (N_RWKV, D, D), D ** -0.5),
        "rwkv_w_v": nrm(ks[22], (N_RWKV, D, D), D ** -0.5),
        "rwkv_w_o": nrm(ks[23], (N_RWKV, D, D), D ** -0.5),
        "rwkv_gn_w": 1.0 + nrm(ks[24], (N_RWKV, D), 0.05),
        "rwkv_gn_b": nrm(ks[25], (N_RWKV, D), 0.01),
        "ffn_w_in": nrm(ks[26], (DEPTH, D, 2 * F), D ** -0.5),
        "ffn_conv_w": nrm(ks[27], (DEPTH, CONV_WIDTH, 2 * F), CONV_WIDTH ** -0.5),
        "ffn_conv_b": nrm(ks[28], (DEPTH, 2 * F), 0.01),
        "ffn_w_out": nrm(ks[29], (DEPTH, F, D), F ** -0.5),
    }

def reference(x, c, mod_w, mod_b, norm_g, fox_w_in, fox_b_f, fox_w_out,
              rwkv_mu, rwkv_w0, rwkv_w1, rwkv_w2, rwkv_a0, rwkv_a1, rwkv_a2,
              rwkv_g1, rwkv_g2, rwkv_k_k, rwkv_k_a, rwkv_r_k,
              rwkv_w_r, rwkv_w_k, rwkv_w_v, rwkv_w_o, rwkv_gn_w, rwkv_gn_b,
              ffn_w_in, ffn_conv_w, ffn_conv_b, ffn_w_out):
    for i in range(DEPTH):
        mod = jax.nn.silu(c) @ mod_w[i] + mod_b[i]
        sh_m, sc_m, g_m, sh_f, sc_f, g_f = [m[:, None, :] for m in jnp.split(mod, 6, axis=-1)]

        h = rms_norm(x, norm_g[i, 0]) * (1 + sc_m) + sh_m
        j = i // N_MIXERS
        if i % N_MIXERS == 0:
            y = fox_attention(h, fox_w_in[j], fox_b_f[j], fox_w_out[j])
        else:
            y = rwkv7_time_mix(h, rwkv_mu[j], rwkv_w0[j], rwkv_w1[j], rwkv_w2[j],
                               rwkv_a0[j], rwkv_a1[j], rwkv_a2[j], rwkv_g1[j], rwkv_g2[j],
                               rwkv_k_k[j], rwkv_k_a[j], rwkv_r_k[j],
                               rwkv_w_r[j], rwkv_w_k[j], rwkv_w_v[j], rwkv_w_o[j],
                               rwkv_gn_w[j], rwkv_gn_b[j])
        x = x + g_m * rms_norm(y, norm_g[i, 1])

        h = rms_norm(x, norm_g[i, 2]) * (1 + sc_f) + sh_f
        y = conv_ffn(h, ffn_w_in[i], ffn_conv_w[i], ffn_conv_b[i], ffn_w_out[i])
        x = x + g_f * rms_norm(y, norm_g[i, 3])
    return x


_drawn_inputs = setup_inputs


def setup_inputs(seed=0):
    import zlib

    import numpy as np

    out = dict(_drawn_inputs(seed))
    spreads = {}
    factors = {'rwkv_w1': 8.0,
     'rwkv_w2': 8.0,
     'rwkv_a0': 4.289,
     'rwkv_a1': 4.235,
     'rwkv_a2': 4.248,
     'rwkv_gn_w': 4.083,
     'rwkv_gn_b': 8.0,
     'ffn_conv_b': 8.0}
    for name, (base, spread) in spreads.items():
        noise = np.random.default_rng([zlib.crc32(name.encode()), seed]).standard_normal(out[name].shape)
        drawn = base * np.exp(spread * noise) if base else spread * noise
        out[name] = __import__('jax').numpy.asarray(drawn.astype(out[name].dtype))
    for name, factor in factors.items():
        out[name] = (out[name] * factor).astype(out[name].dtype)
    return out
```

```python
import math
from contextlib import ExitStack

import numpy as np

import concourse.bass as bass
from concourse import mybir

F32 = mybir.dt.float32
F32R = mybir.dt.float32r
I32 = mybir.dt.int32
ALU = mybir.AluOpType
ACT = mybir.ActivationFunctionType
AX_X = mybir.AxisListType.X
ds = bass.ds

P = 128
D = 2048
S = 256
FF = 5632
KT = D // P
FT = FF // P
TT = S // P
SLAB = 256
NSLAB = D // SLAB
HEADS = 16
LORA = 96
HD = 64
CH = S // HD
NR, NH = 4, 4
PIECE_KT = 4
NORM_EPS, GN_EPS = 1e-6, 64e-5
DECAY_RATE = -math.exp(-0.5)
UP_ITERS = FF // SLAB
DOWN_PIECES = FT // PIECE_KT

C_COND, C_W0, C_A0, C_KK, C_KA, C_RK, C_GNW, C_GNB = range(0, 128, 16)
C_NORM = 128
C_MODB = 256
C_MU = 448
C_CONVW = 544
C_CONVB = C_CONVW + 6 * 2 * FT
C_ALL = C_CONVB + 2 * 2 * FT
MODT = 96

K_ID, K_ONE, K_BLK, K_I64, K_MBK, K_ML, K_EPS = 0, 128, 256, 384, 448, 576, 640
K_MAIN = 644
K_CAUSAL, K_TRIU = K_MAIN, K_MAIN + 384
K_LEVEL = K_TRIU + 512
K_ALL = K_LEVEL + 6 * 128
ROW_COUNTS = [P, P, MODT, MODT, 6 * KT] + [2 * FT] * 8
LEVELS = 6


def shape_constants():
    k = np.zeros((P, K_ALL), np.float32)
    p = np.arange(P)[:, None]
    j = np.arange(P)[None, :]
    h, q = p % HD, np.arange(HD)[None, :]
    k[:, K_ID:K_ID + P] = p == j
    k[:, K_ONE:K_ONE + P] = 1.0
    k[:, K_BLK:K_BLK + P] = p // HD == j // HD
    k[:, K_I64:K_I64 + HD] = h == q
    k[:, K_MBK:K_MBK + HD] = h < q
    k[:, K_MBK + HD:K_MBK + 2 * HD] = h <= q
    k[:, K_ML:K_ML + HD] = q < h
    k[:, K_EPS], k[:, K_EPS + 1] = NORM_EPS, GN_EPS
    k[:, K_CAUSAL:K_CAUSAL + P] = np.where(j <= p, 0.0, -1e30)
    k[:, K_CAUSAL + 2 * P:K_CAUSAL + 3 * P] = np.where(j <= p, 0.0, -1e30)
    t = np.arange(S)[None, :]
    for tile in range(TT):
        k[:, K_TRIU + tile * S:K_TRIU + (tile + 1) * S] = p + tile * P <= t
    for n in range(LEVELS):
        m = 1 << n
        lower = (h // m == q // m + 1) & ((q // m) % 2 == 0)
        upper = (q // m == h // m + 1) & ((h // m) % 2 == 0)
        k[:, K_LEVEL + n * P:K_LEVEL + n * P + HD] = upper
        k[:, K_LEVEL + n * P + HD:K_LEVEL + (n + 1) * P] = lower
    return k


class Phase:
    raw_count = weight_count = unit_count = 0

    def __init__(self, iters, pattern):
        assert len(pattern) % NR == 0 and pattern.count("W") % NH == 0
        assert pattern.count("M") % KT == 0
        self.iters, self.pattern = iters, pattern
        self.raw0, self.w0, self.unit0 = Phase.raw_count, Phase.weight_count, Phase.unit_count
        self.nw, self.units = pattern.count("W"), pattern.count("M") // KT
        Phase.raw_count += iters * len(pattern)
        Phase.weight_count += iters * self.nw
        Phase.unit_count += iters * self.units
        self.w_at = [k for k, c in enumerate(pattern) if c == "W"]
        self.m_at = [k for k, c in enumerate(pattern) if c == "M"]

    def raw(self, k):
        return (self.raw0 + k) % NR

    def landed(self, i, k):
        return i * (16 * len(self.pattern) // NR) + 16 * ((self.raw0 + k) // NR + 1)

    def done(self, i, k):
        return i * len(self.pattern) + (self.raw0 + k + 1)

    def half(self, w):
        return (self.w0 + w) % NH

    def weight(self, i, w):
        return i * self.nw + (self.w0 + w + 1)

    def unit(self, i, u=0):
        return i * self.units + (self.unit0 + u + 1)


class Steps:

    def __init__(self, sem, names, first=""):
        self.sem, self.names, self.first, self.next = sem, names.split(), first.split(), 0
        assert len(set(self.names + self.first)) == len(self.names + self.first), names

    def inc(self, name):
        n = self.next - len(self.first)
        due = self.first[self.next] if n < 0 else self.names[n % len(self.names)]
        assert due == name, (due, name)
        self.next += 1
        return self.sem, 1

    def at(self, name, i=0):
        if name in self.first:
            return self.sem, self.first.index(name) + 1
        return self.sem, i * len(self.names) + (len(self.first) + self.names.index(name) + 1)

    def ended(self, i):
        assert self.first
        return self.sem, i * len(self.names) + len(self.first)


def at_start(i, n):
    return isinstance(i, int) and i == 0 and n <= 0


def spread(w, m):
    out, given = "", 0
    for n in range(w):
        out += "W"
        while given < m * (n + 1) // w:
            out, given = out + "M", given + 1
    return out


def trunk(nc, a, out):
    Phase.raw_count = Phase.weight_count = Phase.unit_count = 0
    ph_mod = Phase(4, "M" * KT)
    ph_fox = Phase(8, spread(12, KT))
    ph_fox_out = Phase(2, spread(16, KT))
    ph_up = [None, None]
    ph_down = [None, None]
    ph_up[0] = Phase(UP_ITERS, "W" * 8)
    ph_down[0] = Phase(2, spread(4 * DOWN_PIECES, 2 * KT))
    ph_lora = Phase(1, "W" * 8)
    ph_rkv = [Phase(4, "W" * 8) for _ in range(3)]
    ph_chunk = Phase(8, "M" * KT)
    ph_rwkv_out = Phase(2, "W" * 16)
    ph_up[1] = Phase(UP_ITERS, "W" * 8)
    ph_down[1] = Phase(2, "W" * (4 * DOWN_PIECES))
    unit_cols = {ph_mod: 1024, ph_fox: 768, ph_fox_out: 1024, ph_down[0]: 1024, ph_chunk: 1024}
    unit_tile0 = {ph_mod: 0, ph_fox: 32, ph_fox_out: 80, ph_down[0]: MODT, ph_chunk: MODT + 32}

    ctx = ExitStack()
    with ctx:
        nsem = [0]

        def sem(name):
            nsem[0] += 1
            return ctx.enter_context(nc.semaphore(name))

        top = nc.sbuf_usable_end
        base = (nc.sbuf_base + 31) // 32 * 32
        O_X = base
        O_XS = O_X + 4 * KT * S
        O_RAW = O_XS + 8 * KT * S
        O_HI = O_RAW + NR * 4096
        O_LO = O_HI + NH * 4096
        O_ACT = O_LO + NH * 4096
        O_SMALL = O_ACT + 8 * FT * S

        def at(name, offset, shape, dt=F32):
            n = 4
            for s in shape[1:]:
                n *= s
            return nc.alloc_sbuf_tensor_at(name, shape, dt, offset=offset), offset + n

        def take(region, name, shape, dt=F32):
            region[0] = (region[0] + 31) // 32 * 32
            t, region[0] = at(name, region[0], shape, dt)
            assert region[0] <= region[1], (name, region)
            return t

        x, _ = at("x", O_X, [P, KT, S])
        xs, _ = at("xs", O_XS, [P, KT, 2, S], F32R)
        y, _ = at("y", O_XS, [P, KT, S])
        sq, _ = at("sq", O_XS + 4 * KT * S, [P, KT, S])
        raw, _ = at("raw", O_RAW, [P, NR, 1024])
        whi, _ = at("whi", O_HI, [P, NH, 4, SLAB], F32R)
        wlo, _ = at("wlo", O_LO, [P, NH, 4, SLAB], F32R)
        act, _ = at("act", O_ACT, [P, FT, 2, S], F32R)
        small = [O_SMALL, top]
        col = take(small, "col", [P, C_ALL])
        con = take(small, "con", [P, K_MAIN])
        mod = take(small, "mod", [P, 2 * MODT])
        cact = take(small, "cact", [P, KT])
        cexp = take(small, "cexp", [P, KT])
        ncol = take(small, "ncol", [P, KT])
        pcol = take(small, "pcol", [P, 4, 2])
        gain_in = take(small, "gain_in", [P, KT])
        gain_out = take(small, "gain_out", [P, KT])
        rs = take(small, "rs", [P, S])
        sqsum = take(small, "sqsum", [P, 2 * S])
        o_macc = small[0] = (small[0] + 31) // 32 * 32
        macc = take(small, "macc", [P, 1024])
        mfin = take(small, "mfin", [P, 1024])
        fend = small[0]
        ub, e = at("ub", o_macc, [P, 4, S + 2])
        tb4, _ = at("tb4", o_macc, [P, 4, S])
        vb, e = at("vb", (e + 31) // 32 * 32, [P, 4, S])
        assert e <= top, (e, top)

        r = [O_ACT, O_SMALL]
        xtok = take(r, "xtok", [P, TT, D])
        crow = take(r, "crow", [P, 13, P])
        r = [O_ACT + 8 * KT * S, O_SMALL]
        wf = take(r, "wf", [P, KT, HEADS])
        wfh = take(r, "wfh", [P, KT, HEADS], F32R)
        wfl = take(r, "wfl", [P, KT, HEADS], F32R)
        bf = take(r, "bf", [1, HEADS])
        gz = take(r, "gz", [P, TT, HEADS])
        ga = take(r, "ga", [P, TT, HEADS])
        gb = take(r, "gb", [P, TT, HEADS])
        gbf = take(r, "gbf", [P, HEADS])
        triu = take(r, "triu", [P, TT, S])
        causal = take(r, "causal", [P, 3 * P])
        negc = take(r, "negc", [HEADS, S])
        nsel = take(r, "nsel", [HEADS, 2, S])
        qf = take(r, "qf", [P, 2, S])
        kf = take(r, "kf", [P, 2, S])
        vt_fox = take(r, "vt_fox", [P, TT, SLAB])
        sm = take(r, "sm", [P, 2, 3 * P])
        ex = take(r, "ex", [P, 2, 3 * P])
        pt = take(r, "pt", [P, 2, 3 * P])
        nmax = take(r, "nmax", [P, 2, 2])
        den = take(r, "den", [P, 2, 2])
        dinv = take(r, "dinv", [P, 2, 2])
        diag = take(r, "diag", [P, 2, 2, P])
        r = [O_ACT, O_ACT + 8 * KT * S]
        hb = take(r, "hb", [P, KT, S + 1])
        dx = take(r, "dx", [P, 2, S])
        mx = take(r, "mx", [P, 4, S])
        r = [O_ACT + 8 * KT * S, O_SMALL]
        rkv = [take(r, n, [P, KT, S]) for n in ("rf", "kfm", "vfm")]
        lvl = take(r, "lvl", [P, LEVELS, P])
        tw = take(r, "tw", [LORA, S])
        ta = take(r, "ta", [LORA, S])
        tg = take(r, "tg", [P, 2, S])
        r1 = [O_XS, O_RAW]
        r2 = [O_HI, O_ACT]
        U = [P, 2, S]
        sig = take(r1, "sig", [P, 2, 2, S])
        dec = take(r1, "dec", U)
        kkr = take(r1, "kkr", U)
        sqk = take(r1, "sqk", U)
        nrm = take(r1, "nrm", U)
        tmpa = take(r1, "tmpa", U)
        kp = take(r1, "kp", U)
        pinv = take(r1, "pinv", U)
        bneg = take(r1, "bneg", U)
        khat = take(r1, "khat", U)
        bonv = take(r1, "bonv", U)
        gate = take(r1, "gate", U)
        zsb = take(r1, "zsb", [P, 2, CH, HD])
        lnm = take(r1, "lnm", [P, 2, CH, HD])
        zero = take(r1, "zero", [P, HD])
        pcum = take(r2, "pcum", [P, 2, CH, HD + 1])
        rr = take(r2, "rr", [P, 2, CH, 2, HD])
        vtok = take(r2, "vtok", [P, 2, CH, HD])
        btok = take(r2, "btok", [P, 2, CH, HD])
        ktok = take(r2, "ktok", [P, 2, CH, HD])
        arb = take(r2, "arb", [P, 2, CH, HD])
        lka = take(r2, "lka", [P, 2, CH, 2, HD])
        ut = take(r2, "ut", [P, 2, CH, 2, HD])
        st = take(r2, "st", [P, 2, 2, HD])
        std = take(r2, "std", [P, 2, HD])
        rhs_s = take(r2, "rhs_s", [P, 2, HD])
        sa = take(r2, "sa", [P, 2, HD])
        lw = take(r2, "lw", [P, 4, SLAB])
        vloc = take(r2, "vloc", U)
        ysb, _ = at("ysb", O_XS, U)
        yc, _ = at("yc", O_XS + 2048, U)
        r = [O_ACT, O_SMALL]
        xout = take(r, "xout", [P, TT, D])

        ps = [ctx.enter_context(nc.psum_tensor(f"ps{b}", [P, 512], F32)) for b in range(8)]
        pmod = ps[7]

        ident, ones, blk = (con[:, k:k + P] for k in (K_ID, K_ONE, K_BLK))
        i64 = con[:, K_I64:K_I64 + HD]
        eps = [con[:, K_EPS:K_EPS + 1], con[:, K_EPS + 1:K_EPS + 2]]

        raw_in = [sem(f"raw_in{n}") for n in range(NR)]
        raw_done = sem("raw_done")
        w_hi = sem("w_hi")
        w_used = sem("w_used")
        mod_summed = sem("mod_summed")
        mod_written = sem("mod_written")
        const_in, rows_in, x_in, fox_in, lvl_in, lw_in, out_done = (
            sem(n) for n in ("const_in", "rows_in", "x_in", "fox_in", "lvl_in", "lw_in", "out_done"))
        NROWS = 20

        def steps(name, names, first=""):
            return Steps(sem(name), names, first)

        groups = range(4)
        se_pe = steps("se_pe", "rows x0 x1 x2 x3 x4 x5 x6 x7")
        se_v = steps("se_v", "cols ncol csum ce cact x0 x1 x2 x3 x4 x5 x6 x7")
        se_a = steps("se_a", "cexp")
        norm = [dict(v=steps(f"norm{n}_v", "gain rinv " + ("t0 t1 t2 t3" if n == 2 else "t0 t1 lo0 t2 lo1 t3 lo2 lo3")),
                     a=steps(f"norm{n}_a", "sq0 sq1 sq2 sq3 root hi0 hi1 hi2 hi3"),
                     pe=steps(f"norm{n}_pe", "sum")) for n in range(4)]
        outp = [dict(a=steps(f"out{n}_a", "y sq"), g=steps(f"out{n}_g", "add"),
                     pe=steps(f"out{n}_pe", "sum"), root=steps(f"out{n}_root", "root"),
                     v=steps(f"out{n}_v", "gain rinv " + " ".join(f"t{g} x{g}" for g in groups)))
                for n in range(4)]
        fg_pe = steps("fg_pe", "z cum")
        fg_a = steps("fg_a", "hi e l")
        fg_v = steps("fg_v", "lo b z abs min ls neg")
        fx_a = steps("fx_a", "q k v")
        at_pe = steps("at_pe", "s t o")
        at_v = steps("at_v", "sel0 sel1 sm0 sm1 m00 m01 m10 m11 rd d00 d01 d10 d11 p0 p1 lo0 lo1")
        at_a = steps("at_a", "e00 e01 e10 e11 hi0 hi1")
        up = [dict(a1=steps(f"up{n}_a1", "u t0 t1 g"), a2=steps(f"up{n}_a2", "u t0 t1 hi"),
                   v1=steps(f"up{n}_v1", "p0 p1 c0 c1"), v2=steps(f"up{n}_v2", "p0 p1 c0 c1 prod lo"),
                   z=steps(f"up{n}_z", "zero")) for n in range(2)]
        lo_pe = steps("lo_pe", "w a g")
        lo_a = steps("lo_a", "tw ta tg")
        mix_v = steps("mix_v", "d0 d1 m0 m1 d2 d3 m2 m3 lo", "zero")
        mix_a = steps("mix_a", "hi")
        rk_a = [steps(f"rk_a{n}", "s0 s1") for n in range(3)]
        z_names = " ".join(f"z{n}p{p}" for n in range(1, LEVELS) for p in range(2))
        u_names = " ".join(f"u{n}p{p}" for n in range(1, LEVELS) for p in range(2))
        pe_names = " ".join(f"z{n}p0 z{n}p1 u{n}p0 u{n}p1" for n in range(1, LEVELS))
        ch_pe = steps("ch_pe", "lora n2 bon vtok btok ktok pb0 pk0 pb1 pk1 ln " + pe_names + " "
                      + " ".join(f"rhs{c} sa{c} m{c} y{c}" for c in range(CH)) + " mean var")
        ch_a = steps("ch_a", "sw0 sw1 sa0 sa1 gate dec nrm vt bt kt " + z_names + " y sqy sd hi")
        ch_v = steps("ch_v", " ".join(f"p{n}" for n in range(8)) + " pinv r1 nmx nrc kkn r0 kka "
                     "bneg khat bonv ub0 arb0 lk0 ub1 arb1 lk1 ln tb " + u_names + " "
                     + " ".join(f"rhs{c} sp{c}a sp{c}b sa{c} st{c}a st{c}b" for c in range(CH))
                     + " yc rs yn gn0 gn1 bo o lo", "zero pone")
        ch_g = steps("ch_g", "c0 c1 c2 c3 k kk0 kk1 sqk t0 t1 kp rk rk0 rk1 v ui st")
        fin_pe = steps("fin_pe", " ".join(f"x{n}" for n in range(8)))
        fin_v = steps("fin_v", " ".join(f"x{n}" for n in range(8)))

        def feat(w):
            return w.rearrange("(k p) n -> p k n", p=P)

        mod_w = [feat(a["mod_w"][n]) for n in range(2)]
        fox_w_in, fox_w_out = feat(a["fox_w_in"][0]), feat(a["fox_w_out"][0])
        w_rkv = [feat(a[n][0]) for n in ("rwkv_w_r", "rwkv_w_k", "rwkv_w_v")]
        w_o = feat(a["rwkv_w_o"][0])
        w_up = [feat(a["ffn_w_in"][n]) for n in range(2)]
        w_down = [feat(a["ffn_w_out"][n]) for n in range(2)]
        w1, a1, g1 = (feat(a[n][0]) for n in ("rwkv_w1", "rwkv_a1", "rwkv_g1"))

        def rows(ap):
            return ap.rearrange("(t p) -> t p", p=P)

        def flat(t):
            return t[:, :, :].rearrange("p a s -> p (a s)")

        def chunks(t):
            return flat(t).rearrange("p (c s) -> p c s", s=HD)

        def chunks_at(t, tile):
            return t[:, ds(tile, 2), :].rearrange("p a (c s) -> p (a c) s", s=HD)

        def pairs(t):
            return t[:, :, :, :].rearrange("p a c s -> p (a c) s")

        def rr_of(u):
            return rr[:, :, :, u, :].rearrange("p a c s -> p (a c) s")

        def mask(k, n):
            return con[:, k:k + HD].unsqueeze(1).broadcast_to([P, n, HD])

        def level(n, u, copies):
            return lvl[:, n, u * HD:(u + 1) * HD].bitcast(I32).unsqueeze(1).broadcast_to([P, copies, HD])

        def shift_col(n, t):
            k = MODT * (n // 2) + 3 * KT * (n % 2) + t
            return mod[:, k:k + 1]

        def waited(engine):
            engine.nop(nofuse=True)

        block = ctx.enter_context(nc.Block())

        @block.sync
        def _(sp):
            def piece(ph, i, k, src, n=None):
                slot = ph.raw(k)
                if not at_start(i, ph.raw0 + k + 1 - NR):
                    sp.wait_ge(raw_done, ph.done(i, k - NR))
                dst = raw[:, slot, :] if n is None else raw[:, slot, 0:n]
                if len(src.shape) == 3 and src.shape[1] > 1:
                    dst = dst.rearrange("p (k n) -> p k n", k=src.shape[1])
                elif len(src.shape) == 3:
                    dst = dst.rearrange("p (k n) -> p k n", k=1)
                sp.dma_start(dst, src).then_inc(raw_in[slot], 16)

            def stream(ph, i, wsrc, layer=0, tile0=0):
                w = m = 0
                cols = unit_cols.get(ph, 0)
                for k, c in enumerate(ph.pattern):
                    if c == "W":
                        piece(ph, i, k, wsrc(w))
                        w += 1
                    else:
                        u, kt = divmod(m, KT)
                        at_col = i * (cols * ph.units) + (tile0 * P + u * cols)
                        piece(ph, i, k, mod_w[layer][:, kt:kt + 1, ds(at_col, cols)], cols)
                        m += 1

            sp.dma_start(con[:, :], a["consts"][:, 0:K_MAIN]).then_inc(const_in, 16)
            n_rows = 0

            def crow_in(b, r0, n, src):
                nonlocal n_rows
                sp.dma_start(crow[r0:r0 + n, b, :], src).then_inc(rows_in, 16)
                n_rows += 1

            crow_in(0, 0, KT, rows(a["c"][0]))
            for n, name in enumerate(("rwkv_w0", "rwkv_a0", "rwkv_k_k", "rwkv_k_a")):
                crow_in(0, KT * (n + 1), KT, rows(a[name][0]))
            crow_in(0, KT * 5, KT, a["rwkv_r_k"][0].rearrange("(t h) n -> t (h n)", h=2))
            crow_in(0, KT * 6, KT, rows(a["rwkv_gn_w"][0]))
            crow_in(0, KT * 7, KT, rows(a["rwkv_gn_b"][0]))
            crow_in(1, 0, P, a["norm_g"].rearrange("l j (t p) -> (l j t) p", p=P))
            for n in range(2):
                crow_in(2 + n, 0, MODT, rows(a["mod_b"][n]))
            crow_in(4, 0, 6 * KT, a["rwkv_mu"][0].rearrange("j (t p) -> (j t) p", p=P))
            for n in range(2):
                for tap in range(3):
                    crow_in(5 + 3 * n + tap, 0, 2 * FT, rows(a["ffn_conv_w"][n, tap]))
                crow_in(11 + n, 0, 2 * FT, rows(a["ffn_conv_b"][n]))
            sp.dma_start(xtok[:, :, :], a["x"][0].rearrange("(t p) d -> p t d", p=P)).then_inc(x_in, 16)
            assert n_rows == NROWS, n_rows
            sp.dma_start(wf[:, :, :], fox_w_in[:, :, 3 * D:3 * D + HEADS]).then_inc(fox_in, 16)
            sp.dma_start(bf[:, :], a["fox_b_f"]).then_inc(fox_in, 16)
            sp.dma_start(triu[:, :, :], a["consts"][:, K_TRIU:K_TRIU + TT * S].rearrange(
                "p (t s) -> p t s", t=TT)).then_inc(fox_in, 16)
            sp.dma_start(causal[:, :], a["consts"][:, K_CAUSAL:K_CAUSAL + 3 * P]).then_inc(fox_in, 16)

            def mod_piece(i, k):
                piece(ph_mod, i, k, mod_w[0][:, k:k + 1, ds(i * 1024, 1024)], 1024)

            for k in range(KT):
                mod_piece(0, k)
            with sp.Fori(1, ph_mod.iters) as i:
                for k in range(KT):
                    mod_piece(i, k)
            with sp.Fori(0, ph_fox.iters) as i:
                stream(ph_fox, i, lambda w: fox_w_in[:, 4 * (w % 4):4 * (w % 4) + 4,
                                                     ds(i * SLAB + (w // 4) * D, SLAB)], 0, 32)

            def out_pieces(ph, wt, per_slab, layer=0, tile0=0):
                with sp.Fori(0, ph.iters) as i:
                    stream(ph, i, lambda w: wt[:, 4 * (w % per_slab):4 * (w % per_slab) + 4,
                                               ds(i * (4 * SLAB) + (w // per_slab) * SLAB, SLAB)], layer, tile0)

            def up_pieces(n):
                with sp.Fori(0, UP_ITERS) as i:
                    stream(ph_up[n], i, lambda w: w_up[n][:, 4 * (w % 4):4 * (w % 4) + 4,
                                                          ds(i * SLAB + (w // 4) * FF, SLAB)])

            out_pieces(ph_fox_out, fox_w_out, 4, 0, 80)
            up_pieces(0)
            out_pieces(ph_down[0], w_down[0], DOWN_PIECES, 1, 0)
            for k in range(2):
                piece(ph_lora, 0, k, w1[:, 8 * k:8 * k + 8, :], 8 * LORA)
            for k in range(2):
                piece(ph_lora, 0, 2 + k, a1[:, 8 * k:8 * k + 8, :], 8 * LORA)
            for k in range(4):
                piece(ph_lora, 0, 4 + k, g1[:, 4 * k:4 * k + 4, :])
            for j in range(3):
                with sp.Fori(0, 4) as i:
                    stream(ph_rkv[j], i, lambda w: w_rkv[j][:, 4 * (w % 4):4 * (w % 4) + 4,
                                                            ds(i * (2 * SLAB) + (w // 4) * SLAB, SLAB)])
            sp.wait_ge(*norm[2]["a"].at("hi3"))
            sp.dma_start(lvl[:, :, :], a["consts"][:, K_LEVEL:K_LEVEL + LEVELS * P].rearrange(
                "p (l s) -> p l s", l=LEVELS)).then_inc(lvl_in, 16)

            def lora_second(i):
                sp.dma_start(lw[0:LORA, 0, :], a["rwkv_w2"][0][:, ds(i * SLAB, SLAB)]).then_inc(lw_in, 16)
                sp.dma_start(lw[0:LORA, 1, :], a["rwkv_a2"][0][:, ds(i * SLAB, SLAB)]).then_inc(lw_in, 16)
                sp.dma_start(lw[:, 2:4, :], a["rwkv_g2"][0].rearrange("(k p) n -> p k n", p=P)[
                    :, :, ds(i * SLAB, SLAB)]).then_inc(lw_in, 16)

            sp.wait_ge(w_used, ph_rkv[2].weight(3, 7))
            lora_second(0)
            stream(ph_chunk, 0, None, 1, 32)
            with sp.Fori(1, ph_chunk.iters) as i:
                sp.wait_ge(*ch_pe.at("lora", i - 1))
                lora_second(i)
                stream(ph_chunk, i, None, 1, 32)
            out_pieces(ph_rwkv_out, w_o, 4)
            up_pieces(1)
            out_pieces(ph_down[1], w_down[1], DOWN_PIECES)
            for t in range(TT):
                sp.wait_ge(*fin_v.at(f"x{4 * t + 3}"))
                sp.dma_start(out[0].rearrange("(t p) d -> p t d", p=P)[:, t, :], xout[:, t, :]).then_inc(out_done, 16)
            sp.wait_ge(out_done, 16 * TT)

        @block.gpsimd
        def _(pool):
            def sum_squares(n):
                o = outp[n]
                for s in range(NSLAB):
                    pool.wait_ge(*o["a"].at("sq", s))
                    src = sq[:, 2 * s:2 * s + 2, :].rearrange("p t s -> p (t s)")
                    if s == 0:
                        pool.tensor_copy(sqsum[:, :], src).then_inc(*o["g"].inc("add"))
                    else:
                        pool.wait_ge(*o["g"].at("add", s - 1))
                        pool.tensor_tensor(sqsum[:, :], sqsum[:, :], src, ALU.add).then_inc(*o["g"].inc("add"))

            sum_squares(0)
            sum_squares(1)
            kf_, g_ = rkv[1], ch_g
            with pool.Fori(0, ph_chunk.iters) as i:
                t0 = i * 2
                pool.wait_ge(*ch_v.ended(i))
                pool.tensor_copy(pcol[:, 0, :], col[:, ds(t0 + C_KK, 2)]).then_inc(*g_.inc("c0"))
                pool.tensor_copy(pcol[:, 1, :], col[:, ds(t0 + C_KA, 2)]).then_inc(*g_.inc("c1"))
                pool.tensor_copy(pcol[:, 2, :], ncol[:, ds(t0, 2)]).then_inc(*g_.inc("c2"))
                pool.tensor_copy(pcol[:, 3, :], col[:, ds(t0 + C_RK, 2)]).then_inc(*g_.inc("c3"))
                pool.tensor_copy(kkr[:, :, :], kf_[:, ds(t0, 2), :]).then_inc(*g_.inc("k"))
                pool.wait_ge(*g_.at("k", i))
                waited(pool)
                for p in range(2):
                    pool.tensor_scalar(kkr[:, p, :], kkr[:, p, :], pcol[:, 0, p:p + 1], None,
                                       ALU.mult).then_inc(*g_.inc(f"kk{p}"))
                pool.wait_ge(*g_.at("kk1", i))
                pool.tensor_tensor(sqk[:, :, :], kkr[:, :, :], kkr[:, :, :], ALU.mult).then_inc(*g_.inc("sqk"))
                for p in range(2):
                    pool.wait_ge(*ch_a.at(f"sa{p}", i))
                    waited(pool)
                    pool.tensor_scalar(tmpa[:, p, :], sig[:, 1, p, :], pcol[:, 1, p:p + 1], pcol[:, 2, p:p + 1],
                                       ALU.mult, ALU.add).then_inc(*g_.inc(f"t{p}"))
                pool.wait_ge(*g_.at("t1", i))
                waited(pool)
                pool.tensor_tensor(kp[:, :, :], tmpa[:, :, :], kf_[:, ds(t0, 2), :], ALU.mult).then_inc(*g_.inc("kp"))
                pool.wait_ge(*g_.at("kp", i))
                pool.wait_ge(*ch_v.at("p7", i))
                waited(pool)
                pool.tensor_tensor(dec[:, :, :], kp[:, :, :], rkv[0][:, ds(t0, 2), :], ALU.mult).then_inc(*g_.inc("rk"))
                pool.wait_ge(*g_.at("rk", i))
                waited(pool)
                for p in range(2):
                    pool.tensor_scalar(dec[:, p, :], dec[:, p, :], pcol[:, 3, p:p + 1],
                                       None, ALU.mult).then_inc(*g_.inc(f"rk{p}"))
                pool.tensor_copy(vloc[:, :, :], rkv[2][:, ds(t0, 2), :]).then_inc(*g_.inc("v"))
                pool.tensor_copy(ut[:, :, :, :, :].rearrange("p a c u s -> p (a c u) s"),
                                 i64.unsqueeze(1).broadcast_to([P, 2 * CH * 2, HD])).then_inc(*g_.inc("ui"))
                pool.memset(st[:, 0, :, :], 0.0).then_inc(*g_.inc("st"))
            sum_squares(2)
            sum_squares(3)

        @block.scalar
        def _(sc):
            def hi(ph, i, w):
                k = ph.w_at[w]
                slot, half = ph.raw(k), ph.half(w)
                sc.wait_ge(raw_in[slot], ph.landed(i, k))
                if not at_start(i, ph.w0 + w + 1 - NH):
                    sc.wait_ge(w_used, ph.weight(i, w - NH))
                sc.activation(whi[:, half, :, :].rearrange("p k n -> p (k n)"), raw[:, slot, :],
                              ACT.Copy).then_inc(w_hi, 1)

            def laps(n, body):
                body(0, True)
                with sc.Fori(1, n) as i:
                    body(i, False)

            def x_squares(n, x_ready):
                s = norm[n]
                for g in groups:
                    sc.wait_ge(*x_ready(g))
                    sc.activation(sq[:, 4 * g:4 * g + 4, :], x[:, 4 * g:4 * g + 4, :], ACT.Square).then_inc(
                        *s["a"].inc(f"sq{g}"))
                sc.wait_ge(*s["pe"].at("sum"))
                sc.activation(rs[:, :], ps[5][:, 0:S], ACT.Sqrt, bias=eps[0], scale=1.0 / D).then_inc(*s["a"].inc("root"))
                for g in groups:
                    sc.wait_ge(*s["v"].at(f"t{g}"))
                    src = (vb if g % 2 else tb4)
                    for t in range(4 * g, 4 * g + 4):
                        dst = hb[:, t, 1:S + 1] if n == 2 else xs[:, t, 0, :]
                        last = sc.activation(dst, src[:, t % 4, :], ACT.Identity, bias=shift_col(n, t))
                    last.then_inc(*s["a"].inc(f"hi{g}"))

            def out_proj(n, ph, per_slab):
                o = outp[n]

                def result(i, s):
                    slab = i * 4 + s
                    sc.wait_ge(w_used, ph.weight(i, (s + 1) * per_slab - 1))
                    src = ps[s][:, :].rearrange("p (m t) -> p m t", m=2)
                    sc.activation(y[:, ds(slab * 2, 2), :], src, ACT.Copy).then_inc(*o["a"].inc("y"))
                    sc.activation(sq[:, ds(slab * 2, 2), :], src, ACT.Square).then_inc(*o["a"].inc("sq"))

                with sc.Fori(0, ph.iters) as i:
                    for s in range(4):
                        for q in range(per_slab):
                            hi(ph, i, s * per_slab + q)
                            if s and q == 1:
                                result(i, s - 1)
                    result(i, 3)
                sc.wait_ge(*o["pe"].at("sum"))
                sc.activation(rs[:, :], ps[4][:, 0:S], ACT.Sqrt, bias=eps[0], scale=1.0 / D).then_inc(
                    *o["root"].inc("root"))

            sc.wait_ge(*se_v.at("cols"))
            sc.activation(cexp[:, :], col[:, C_COND:C_COND + KT], ACT.Exp, scale=-1.0).then_inc(*se_a.inc("cexp"))

            x_squares(0, lambda g: se_v.at(f"x{2 * g + 1}"))
            sc.wait_ge(fox_in, 64)
            sc.activation(wfh[:, :, :], wf[:, :, :], ACT.Copy).then_inc(*fg_a.inc("hi"))

            def fox_q(i):
                sc.wait_ge(w_used, ph_fox.weight(i, 3))
                sc.activation(qf[:, :, :], ps[0][:, :].rearrange("p (m t) -> p m t", m=2), ACT.Copy,
                              scale=float(P) ** -0.5).then_inc(*fx_a.inc("q"))

            def fox_k(i):
                sc.wait_ge(w_used, ph_fox.weight(i, 7))
                sc.activation(kf[:, :, :], ps[1][:, :].rearrange("p (m t) -> p m t", m=2),
                              ACT.Copy).then_inc(*fx_a.inc("k"))

            def fox_v(i):
                sc.wait_ge(w_used, ph_fox.weight(i, 11))
                sc.activation(vt_fox[:, :, :], ps[2][:, :].rearrange("p (m t) -> p m t", m=2),
                              ACT.Copy).then_inc(*fx_a.inc("v"))

            def softmax_exp(a_):
                sc.wait_ge(*at_v.at("m11", a_))
                for h in range(2):
                    for t in range(2):
                        lo_, hi_ = (0, P) if t == 0 else (P, 3 * P)
                        sc.activation(ex[:, h, lo_:hi_], sm[:, h, lo_:hi_], ACT.Exp, bias=nmax[:, h, t:t + 1],
                                      accum_out=den[:, h, t:t + 1]).then_inc(*at_a.inc(f"e{h}{t}"))

            def attn_hi(a_):
                sc.wait_ge(*at_pe.at("o", a_))
                for h in range(2):
                    sc.activation(act[:, ds(a_ * 2 + h, 1), 0, :].rearrange("p a s -> p (a s)"), ps[3 + h][:, 0:S],
                                  ACT.Copy).then_inc(*at_a.inc(f"hi{h}"))

            def fox_body(i, first):
                for w in range(12):
                    hi(ph_fox, i, w)
                    if w == 1 and not first:
                        fox_v(i - 1)
                        softmax_exp(i - 1)
                    if w == 5:
                        fox_q(i)
                        if first:
                            sc.wait_ge(*fg_v.at("abs"))
                            sc.activation(gb[:, :, :], ga[:, :, :], ACT.Exp, scale=-1.0).then_inc(*fg_a.inc("e"))
                            sc.wait_ge(*fg_a.at("e"))
                            sc.activation(gb[:, :, :], gb[:, :, :], ACT.Ln, bias=con[:, K_ONE:K_ONE + 1]).then_inc(
                                *fg_a.inc("l"))
                    if w == 9:
                        fox_k(i)
                        if not first:
                            attn_hi(i - 1)

            laps(8, fox_body)
            fox_v(7)
            softmax_exp(7)
            attn_hi(7)
            out_proj(0, ph_fox_out, 4)

            def up_proj(n):
                ph, s = ph_up[n], up[n]

                def taps(i, half, steps_):
                    sc.wait_ge(w_used, ph.weight(i, 4 * half + 3))
                    src = ps[half][:, :].rearrange("p (m t) -> p m t", m=2)
                    sc.activation(ub[:, 2 * half:2 * half + 2, 2:S + 2], src, ACT.Copy).then_inc(*steps_.inc("u"))
                    for m in range(2):
                        c = i * 2 + (half * FT + m)
                        sc.activation(vb[:, 2 * half + m, :], src[:, m, :], ACT.Identity,
                                      bias=col[:, ds(c + (C_CONVB + 2 * FT * n), 1)],
                                      scale=col[:, ds(c + (C_CONVW + 2 * FT * (3 * n + 2)), 1)]).then_inc(
                                          *steps_.inc(f"t{m}"))

                def first_half(i):
                    taps(i, 0, s["a1"])
                    sc.wait_ge(*s["v1"].at("c1", i))
                    sc.activation(vb[:, 0:2, :], vb[:, 0:2, :], ACT.Gelu).then_inc(*s["a1"].inc("g"))

                def second_half(i):
                    taps(i, 1, s["a2"])
                    sc.wait_ge(*s["v2"].at("prod", i))
                    sc.activation(act[:, ds(i * 2, 2), 0, :], vb[:, 2:4, :], ACT.Copy).then_inc(*s["a2"].inc("hi"))

                def body(i, first):
                    for w in range(8):
                        hi(ph, i, w)
                        if w == 1 and not first:
                            second_half(i - 1)
                        if w == 5:
                            if first:
                                sc.wait_ge(*s["z"].at("zero"))
                            first_half(i)

                laps(UP_ITERS, body)
                second_half(UP_ITERS - 1)

            x_squares(1, lambda g: outp[0]["v"].at(f"x{g}"))
            up_proj(0)
            out_proj(1, ph_down[0], DOWN_PIECES)
            x_squares(2, lambda g: outp[1]["v"].at(f"x{g}"))

            def mix_hi(j):
                with sc.Fori(0, 4) as i:
                    sc.wait_ge(*mix_v.at("m3", i + 4 * j))
                    sc.activation(xs[:, ds(i * 4, 4), 0, :], mx[:, :, :], ACT.Copy).then_inc(*mix_a.inc("hi"))

            for j, (w0_, nw_, func, dst, src) in enumerate((
                    (0, 2, ACT.Tanh, tw[:, :], ps[4][0:LORA, 0:S]),
                    (2, 2, ACT.Copy, ta[:, :], ps[5][0:LORA, 0:S]),
                    (4, 4, ACT.Sigmoid, tg[:, :, :], ps[6][:, :].rearrange("p (m t) -> p m t", m=2)))):
                mix_hi(j)
                for w in range(w0_, w0_ + nw_):
                    hi(ph_lora, 0, w)
                sc.wait_ge(w_used, ph_lora.weight(0, w0_ + nw_ - 1))
                sc.activation(dst, src, func).then_inc(*lo_a.inc(("tw", "ta", "tg")[j]))
            for j in range(3):
                mix_hi(3 + j)

                def result(i, s):
                    sc.wait_ge(w_used, ph_rkv[j].weight(i, 4 * s + 3))
                    sc.activation(rkv[j][:, ds(i * 4 + 2 * s, 2), :], ps[s][:, :].rearrange("p (m t) -> p m t", m=2),
                                  ACT.Copy).then_inc(*rk_a[j].inc(f"s{s}"))

                def rkv_body(i, first):
                    for w in range(8):
                        hi(ph_rkv[j], i, w)
                        if w == 1 and not first:
                            result(i - 1, 1)
                        if w == 5:
                            result(i, 0)

                laps(4, rkv_body)
                result(3, 1)

            sc.wait_ge(*ch_v.at("pone"))
            with sc.Fori(0, ph_chunk.iters) as i:
                t0 = i * 2
                sc.wait_ge(*ch_v.ended(i))
                sc.wait_ge(*ch_pe.at("lora", i))
                for b, (nm, c0) in enumerate((("sw", C_W0), ("sa", C_A0))):
                    for p in range(2):
                        sc.activation(sig[:, b, p, :], ps[b][:, p * S:p * S + S], ACT.Sigmoid,
                                      bias=col[:, ds(t0 + (c0 + p), 1)]).then_inc(*ch_a.inc(f"{nm}{p}"))
                sc.activation(flat(gate), ps[2][:, :], ACT.Copy).then_inc(*ch_a.inc("gate"))
                sc.wait_ge(*ch_a.at("sw1", i))
                sc.activation(dec[:, :, :], sig[:, 0, :, :], ACT.Exp, scale=DECAY_RATE).then_inc(*ch_a.inc("dec"))
                sc.wait_ge(*ch_pe.at("n2", i))
                sc.activation(flat(nrm), ps[3][:, :], ACT.Sqrt).then_inc(*ch_a.inc("nrm"))
                for nm, dst, b in (("v", vtok, 5), ("b", btok, 6), ("k", ktok, 0)):
                    sc.wait_ge(*ch_pe.at(f"{nm}tok", i))
                    sc.activation(dst[:, :, :, :].rearrange("p a c s -> p (a c s)"), ps[b][:, :],
                                  ACT.Copy).then_inc(*ch_a.inc(f"{nm}t"))
                for n in range(1, LEVELS):
                    for p in range(2):
                        sc.wait_ge(*ch_pe.at(f"z{n}p{p}", i))
                        sc.activation(zsb[:, p, :, :].rearrange("p c s -> p (c s)"), ps[p][:, 0:S],
                                      ACT.Copy).then_inc(*ch_a.inc(f"z{n}p{p}"))
                sc.wait_ge(*ch_pe.at(f"y{CH - 1}", i))
                sc.activation(flat(ysb), ps[0][:, :], ACT.Copy).then_inc(*ch_a.inc("y"))
                sc.wait_ge(*ch_v.at("yc", i))
                sc.activation(sqk[:, :, :], yc[:, :, :], ACT.Square).then_inc(*ch_a.inc("sqy"))
                sc.wait_ge(*ch_pe.at("var", i))
                sc.activation(flat(nrm), ps[2][:, :], ACT.Sqrt, bias=eps[1], scale=1.0 / HD).then_inc(*ch_a.inc("sd"))
                sc.wait_ge(*ch_v.at("o", i))
                sc.activation(act[:, ds(t0, 2), 0, :], tmpa[:, :, :], ACT.Copy).then_inc(*ch_a.inc("hi"))
            out_proj(2, ph_rwkv_out, 4)
            x_squares(3, lambda g: outp[2]["v"].at(f"x{g}"))
            up_proj(1)
            out_proj(3, ph_down[1], DOWN_PIECES)

        @block.vector
        def _(v):
            def lo(ph, i, w):
                k = ph.w_at[w]
                slot, half = ph.raw(k), ph.half(w)
                v.wait_ge(w_hi, ph.weight(i, w))
                v.tensor_tensor(wlo[:, half, :, :].rearrange("p k n -> p (k n)"), raw[:, slot, :],
                                whi[:, half, :, :].rearrange("p k n -> p (k n)").bitcast(F32),
                                ALU.subtract).then_inc(raw_done, 1)

            def adaln(ph, i, m):
                k = ph.m_at[m]
                slot, cols = ph.raw(k), unit_cols[ph]
                u, kt = divmod(m, KT)
                v.wait_ge(raw_in[slot], ph.landed(i, k))
                if kt == 0:
                    if ph is ph_mod:
                        v.wait_ge(*se_v.at("cact"))
                    if not at_start(i, ph.raw0 + k):
                        v.wait_ge(raw_done, ph.done(i, k - 1))
                    v.tensor_scalar(macc[:, 0:cols], raw[:, slot, 0:cols], cact[:, 0:1], None,
                                    ALU.mult).then_inc(raw_done, 1)
                    return
                v.wait_ge(raw_done, ph.done(i, ph.m_at[m - 1]))
                if kt == KT - 1 and not at_start(i, ph.unit0 + u):
                    v.wait_ge(mod_summed, ph.unit(i, u - 1))
                v.scalar_tensor_tensor(mfin[:, 0:cols] if kt == KT - 1 else macc[:, 0:cols], raw[:, slot, 0:cols],
                                       cact[:, kt:kt + 1], macc[:, 0:cols], ALU.mult, ALU.add).then_inc(raw_done, 1)

            def adaln_out(ph, i, u=0):
                n = unit_cols[ph] // P
                t = i * (n * ph.units) + (unit_tile0[ph] + u * n)
                v.wait_ge(mod_summed, ph.unit(i, u))
                v.tensor_tensor(mod[:, ds(t, n)], pmod[:, 0:n], col[:, ds(t + C_MODB, n)], ALU.add).then_inc(mod_written, 1)

            def pieces(ph, i, hooks=None):
                w = m = 0
                for c in ph.pattern:
                    if c == "W":
                        lo(ph, i, w)
                        if hooks and w in hooks:
                            hooks[w]()
                        w += 1
                    else:
                        adaln(ph, i, m)
                        m += 1

            def laps(n, body):
                body(0, True)
                with v.Fori(1, n) as i:
                    body(i, False)

            def x_norm(n):
                s = norm[n]
                layer, which = divmod(n, 2)
                scale = MODT * layer + 3 * KT * which + KT
                v.wait_ge(mod_written, (ph_mod.unit(3), ph_fox.unit(7), ph_down[0].unit(1, 1), ph_chunk.unit(7))[n])
                v.scalar_tensor_tensor(gain_in[:, :], mod[:, scale:scale + KT], 1.0,
                                       col[:, C_NORM + 64 * layer + 32 * which:C_NORM + 64 * layer + 32 * which + KT],
                                       ALU.add, ALU.mult).then_inc(*s["v"].inc("gain"))
                v.wait_ge(*s["a"].at("root"))
                v.reciprocal(rs[:, :], rs[:, :]).then_inc(*s["v"].inc("rinv"))
                v.wait_ge(*s["v"].at("rinv"))
                for g in range(5):
                    if g < 4:
                        buf = vb if g % 2 else tb4
                        if g >= 2 and n == 2:
                            v.wait_ge(*s["a"].at(f"hi{g - 2}"))
                        if g >= 2 and n != 2:
                            v.wait_ge(*s["v"].at(f"lo{g - 2}"))
                        for t in range(4 * g, 4 * g + 4):
                            last = v.scalar_tensor_tensor(buf[:, t % 4, :], x[:, t, :], gain_in[:, t:t + 1], rs[:, :],
                                                          ALU.mult, ALU.mult)
                        last.then_inc(*s["v"].inc(f"t{g}"))
                    if g >= 1 and n != 2:
                        h = g - 1
                        buf = vb if h % 2 else tb4
                        v.wait_ge(*s["a"].at(f"hi{h}"))
                        for t in range(4 * h, 4 * h + 4):
                            last = v.scalar_tensor_tensor(xs[:, t, 1, :], buf[:, t % 4, :], shift_col(n, t),
                                                          xs[:, t, 0, :].bitcast(F32), ALU.add, ALU.subtract)
                        last.then_inc(*s["v"].inc(f"lo{h}"))
                if n == 2:
                    v.wait_ge(*s["a"].at("hi3"))
                    v.wait_ge(*s["v"].at("t3"))
                else:
                    v.wait_ge(*s["v"].at("lo3"))

            def residual(n):
                o = outp[n]
                layer, which = divmod(n, 2)
                gt = MODT * layer + 3 * KT * which + 2 * KT
                g0 = C_NORM + 64 * layer + 32 * which + KT
                v.wait_ge(mod_written, (ph_fox.unit(7), ph_fox_out.unit(1), ph_chunk.unit(7), ph_chunk.unit(7))[n])
                v.tensor_tensor(gain_out[:, :], mod[:, gt:gt + KT], col[:, g0:g0 + KT], ALU.mult).then_inc(
                    *o["v"].inc("gain"))
                v.wait_ge(*o["root"].at("root"))
                v.reciprocal(rs[:, :], rs[:, :]).then_inc(*o["v"].inc("rinv"))
                v.wait_ge(*o["v"].at("rinv"))
                for g in groups:
                    for t in range(4 * g, 4 * g + 4):
                        last = v.scalar_tensor_tensor(y[:, t, :], y[:, t, :], gain_out[:, t:t + 1], rs[:, :],
                                                      ALU.mult, ALU.mult)
                    last.then_inc(*o["v"].inc(f"t{g}"))
                    v.wait_ge(*o["v"].at(f"t{g}"))
                    v.tensor_tensor(x[:, 4 * g:4 * g + 4, :], x[:, 4 * g:4 * g + 4, :], y[:, 4 * g:4 * g + 4, :],
                                    ALU.add).then_inc(*o["v"].inc(f"x{g}"))
                v.wait_ge(*o["v"].at("x3"))

            v.wait_ge(*se_pe.at("rows"))
            at_col = 0
            for b, n in enumerate(ROW_COUNTS):
                last = v.tensor_copy(col[:, at_col:at_col + n], ps[b // 4][:, (b % 4) * P:(b % 4) * P + n])
                at_col += n
            assert at_col == C_ALL
            last.then_inc(*se_v.inc("cols"))
            v.wait_ge(*se_v.at("cols"))
            v.tensor_scalar(ncol[:, :], col[:, C_KA:C_KA + KT], -1.0, 1.0, ALU.mult, ALU.add).then_inc(*se_v.inc("ncol"))
            v.wait_ge(*se_a.at("cexp"))
            v.tensor_scalar(cexp[:, :], cexp[:, :], 1.0, None, ALU.add).then_inc(*se_v.inc("csum"))
            v.wait_ge(*se_v.at("csum"))
            v.reciprocal(cexp[:, :], cexp[:, :]).then_inc(*se_v.inc("ce"))
            v.wait_ge(*se_v.at("ce"))
            v.tensor_tensor(cact[:, :], cexp[:, :], col[:, C_COND:C_COND + KT], ALU.mult).then_inc(*se_v.inc("cact"))
            for g in range(8):
                v.wait_ge(*se_pe.at(f"x{g}"))
                v.tensor_copy(x[:, 2 * g:2 * g + 2, :], ps[4 + g % 3][:, :].rearrange("p (m t) -> p m t", m=2)).then_inc(
                    *se_v.inc(f"x{g}"))

            def mod_body(i, first):
                for m in range(KT):
                    adaln(ph_mod, i, m)
                adaln_out(ph_mod, i)

            laps(4, mod_body)
            x_norm(0)

            v.wait_ge(*fg_a.at("hi"))
            v.tensor_tensor(wfl[:, :, :], wf[:, :, :], wfh[:, :, :].bitcast(F32), ALU.subtract).then_inc(*fg_v.inc("lo"))

            def gate_first():
                v.wait_ge(*fg_pe.at("z"))
                v.tensor_copy(gbf[:, :], ps[3][:, 32:32 + HEADS]).then_inc(*fg_v.inc("b"))
                v.wait_ge(*fg_v.at("b"))
                v.tensor_tensor(gz[:, :, :], ps[3][:, 0:TT * HEADS].rearrange("p (t h) -> p t h", t=TT),
                                gbf[:, :].unsqueeze(1).broadcast_to([P, TT, HEADS]), ALU.add).then_inc(*fg_v.inc("z"))
                v.wait_ge(*fg_v.at("z"))
                v.scalar_tensor_tensor(ga[:, :, :], gz[:, :, :], -1.0, gz[:, :, :], ALU.mult, ALU.max).then_inc(
                    *fg_v.inc("abs"))

            def gate_second():
                v.wait_ge(*fg_a.at("l"))
                v.tensor_scalar(ga[:, :, :], gz[:, :, :], 0.0, None, ALU.min).then_inc(*fg_v.inc("min"))
                v.wait_ge(*fg_v.at("min"))
                v.tensor_tensor(ga[:, :, :], ga[:, :, :], gb[:, :, :], ALU.subtract).then_inc(*fg_v.inc("ls"))

            def select(a_):
                for h in range(2):
                    v.tensor_scalar(nsel[:, h, :], negc[:, :], con[0:HEADS, ds(a_ * 2 + (K_ID + h), 1)], None,
                                    ALU.mult).then_inc(*at_v.inc(f"sel{h}"))

            def softmax_max(a_):
                v.wait_ge(*at_pe.at("s", a_))
                for h in range(2):
                    v.tensor_tensor(sm[:, h, :], ps[3 + h][:, 0:3 * P], causal[:, :], ALU.add).then_inc(
                        *at_v.inc(f"sm{h}"))
                for h in range(2):
                    v.wait_ge(*at_v.at(f"sm{h}", a_))
                    for t in range(2):
                        lo_, hi_ = (0, P) if t == 0 else (P, 3 * P)
                        v.tensor_reduce(nmax[:, h, t:t + 1], sm[:, h, lo_:hi_], AX_X, ALU.max,
                                        negate=True).then_inc(*at_v.inc(f"m{h}{t}"))

            def softmax_den(a_):
                v.wait_ge(*at_a.at("e11", a_))
                v.reciprocal(dinv[:, :, :], den[:, :, :]).then_inc(*at_v.inc("rd"))
                v.wait_ge(*at_v.at("rd", a_))
                for h in range(2):
                    for t in range(2):
                        v.tensor_scalar(diag[:, h, t, :], ident, dinv[:, h, t:t + 1], None,
                                        ALU.mult).then_inc(*at_v.inc(f"d{h}{t}"))

            def probs_out(a_):
                v.wait_ge(*at_pe.at("t", a_))
                for h in range(2):
                    v.tensor_copy(pt[:, h, :], ps[5 + h][:, 0:3 * P]).then_inc(*at_v.inc(f"p{h}"))

            def attn_lo(a_):
                for h in range(2):
                    v.wait_ge(*at_a.at(f"hi{h}", a_))
                    v.tensor_tensor(act[:, ds(a_ * 2 + h, 1), 1, :].rearrange("p a s -> p (a s)"), ps[3 + h][:, 0:S],
                                    act[:, ds(a_ * 2 + h, 1), 0, :].rearrange("p a s -> p (a s)").bitcast(F32),
                                    ALU.subtract).then_inc(*at_v.inc(f"lo{h}"))

            def fox_body(i, first):
                if first:
                    pieces(ph_fox, i, {5: gate_first, 7: gate_second})
                    v.wait_ge(*fg_pe.at("cum"))
                    v.tensor_scalar(negc[:, :], ps[3][0:HEADS, P:P + S], -1.0, None, ALU.mult).then_inc(
                        *fg_v.inc("neg"))
                    v.wait_ge(*fg_v.at("neg"))
                else:
                    pieces(ph_fox, i, {1: lambda: softmax_max(i - 1), 2: lambda: softmax_den(i - 1),
                                       3: lambda: adaln_out(ph_fox, i - 1), 5: lambda: probs_out(i - 1),
                                       9: lambda: attn_lo(i - 1)})
                select(i)

            laps(8, fox_body)
            softmax_max(7)
            softmax_den(7)
            adaln_out(ph_fox, 7)
            probs_out(7)
            attn_lo(7)

            def out_proj(n, ph, per_slab):
                with v.Fori(0, ph.iters) as i:
                    hooks = {3 * per_slab + 6: lambda: adaln_out(ph, i, 0)} if ph.units == 2 else None
                    pieces(ph, i, hooks)
                    if ph.units:
                        adaln_out(ph, i, ph.units - 1)
                residual(n)

            out_proj(0, ph_fox_out, 4)

            def up_proj(n):
                ph, s = ph_up[n], up[n]
                v.memset(ub[:, :, 0:2], 0.0).then_inc(*s["z"].inc("zero"))

                def conv(i, half, a_, st_):
                    v.wait_ge(*a_.at("t1", i))
                    for tap, nm in ((1, "p"), (0, "c")):
                        for m in range(2):
                            if tap == 0:
                                v.wait_ge(*st_.at(f"p{m}", i))
                            c = i * 2 + (half * FT + m + C_CONVW + 2 * FT * (3 * n + tap))
                            q = 2 * half + m
                            v.scalar_tensor_tensor(vb[:, q, :], ub[:, q, tap:tap + S], col[:, ds(c, 1)], vb[:, q, :],
                                                   ALU.mult, ALU.add).then_inc(*st_.inc(f"{nm}{m}"))

                def second_half(i):
                    conv(i, 1, s["a2"], s["v2"])
                    v.wait_ge(*s["a1"].at("g", i))
                    v.wait_ge(*s["v2"].at("c1", i))
                    v.tensor_tensor(vb[:, 2:4, :], vb[:, 2:4, :], vb[:, 0:2, :], ALU.mult).then_inc(
                        *s["v2"].inc("prod"))
                    v.wait_ge(*s["a2"].at("hi", i))
                    v.tensor_tensor(act[:, ds(i * 2, 2), 1, :], vb[:, 2:4, :],
                                    act[:, ds(i * 2, 2), 0, :].bitcast(F32), ALU.subtract).then_inc(*s["v2"].inc("lo"))

                def body(i, first):
                    hooks = {5: lambda: conv(i, 0, s["a1"], s["v1"])}
                    if not first:
                        hooks[1] = lambda: second_half(i - 1)
                    pieces(ph, i, hooks)

                laps(UP_ITERS, body)
                second_half(UP_ITERS - 1)
                v.wait_ge(*s["v2"].at("lo", UP_ITERS - 1))

            x_norm(1)
            up_proj(0)
            out_proj(1, ph_down[0], DOWN_PIECES)
            x_norm(2)

            v.memset(hb[:, :, 0:1], 0.0).then_inc(*mix_v.inc("zero"))

            def mix(j, which, used):
                if used:
                    v.wait_ge(w_used, used)
                with v.Fori(0, 4) as i:
                    r_ = i + 4 * j
                    v.wait_ge(*mix_v.ended(r_))
                    for n0 in (0, 2):
                        for t in (n0, n0 + 1):
                            if n0:
                                v.wait_ge(*mix_v.at(f"m{t - 2}", r_))
                            v.tensor_tensor(dx[:, t % 2, :], hb[:, ds(i * 4 + t, 1), 0:S].rearrange("p a s -> p (a s)"),
                                            hb[:, ds(i * 4 + t, 1), 1:S + 1].rearrange("p a s -> p (a s)"),
                                            ALU.subtract).then_inc(*mix_v.inc(f"d{t}"))
                        for t in (n0, n0 + 1):
                            v.wait_ge(*mix_v.at(f"d{t}", r_))
                            v.scalar_tensor_tensor(mx[:, t, :], dx[:, t % 2, :],
                                                   col[:, ds(i * 4 + (C_MU + KT * which + t), 1)],
                                                   hb[:, ds(i * 4 + t, 1), 1:S + 1].rearrange("p a s -> p (a s)"),
                                                   ALU.mult, ALU.add).then_inc(*mix_v.inc(f"m{t}"))
                    v.wait_ge(*mix_a.at("hi", r_))
                    v.tensor_tensor(xs[:, ds(i * 4, 4), 1, :], mx[:, :, :], xs[:, ds(i * 4, 4), 0, :].bitcast(F32),
                                    ALU.subtract).then_inc(*mix_v.inc("lo"))

            for j, (which, w0_, nw_) in enumerate(((1, 0, 2), (4, 2, 2), (5, 4, 4))):
                mix(j, which, ph_lora.weight(0, w0_ - 1) if j else 0)
                for w in range(w0_, w0_ + nw_):
                    lo(ph_lora, 0, w)
            for j, which in enumerate((0, 2, 3)):
                mix(3 + j, which, ph_rkv[j - 1].weight(3, 7) if j else ph_lora.weight(0, 7))
                with v.Fori(0, 4) as i:
                    pieces(ph_rkv[j], i)

            v.wait_ge(w_used, ph_rkv[2].weight(3, 7))
            v.wait_ge(*rk_a[2].at("s1", 3))
            v.wait_ge(lvl_in, 16)
            v.memset(zero[:, :], 0.0).then_inc(*ch_v.inc("zero"))
            v.memset(pcum[:, :, :, 0:1], 1.0).then_inc(*ch_v.inc("pone"))
            with v.Fori(0, ph_chunk.iters) as i:
                t0, c_ = i * 2, ch_v
                m_ = [0]

                def some(n):
                    for _ in range(n):
                        adaln(ph_chunk, i, m_[0])
                        m_[0] += 1

                v.wait_ge(*c_.ended(i))
                v.wait_ge(*ch_a.at("dec", i))
                for n in range(8):
                    p, c = divmod(n, CH)
                    v.tensor_tensor_scan(pcum[:, p, c, 1:HD + 1], dec[:, p, c * HD:c * HD + HD], zero[:, :], 1.0,
                                         ALU.mult, ALU.add).then_inc(*c_.inc(f"p{n}"))
                v.wait_ge(*c_.at("p7", i))
                v.reciprocal(chunks(pinv), pairs(pcum)[:, :, 1:HD + 1]).then_inc(*c_.inc("pinv"))
                v.tensor_tensor(rr_of(1), chunks_at(rkv[0], t0), pairs(pcum)[:, :, 1:HD + 1], ALU.mult).then_inc(
                    *c_.inc("r1"))
                v.wait_ge(*ch_a.at("nrm", i))
                v.tensor_scalar(flat(nrm), flat(nrm), 1e-12, None, ALU.max).then_inc(*c_.inc("nmx"))
                v.wait_ge(*c_.at("nmx", i))
                v.reciprocal(flat(nrm), flat(nrm)).then_inc(*c_.inc("nrc"))
                v.wait_ge(*c_.at("nrc", i))
                v.wait_ge(*ch_g.at("sqk", i))
                v.tensor_tensor(flat(kkr), flat(kkr), flat(nrm), ALU.mult).then_inc(*c_.inc("kkn"))
                v.wait_ge(*c_.at("kkn", i))
                v.tensor_tensor(rr_of(0), chunks(kkr), pairs(pcum)[:, :, 0:HD], ALU.mult).then_inc(*c_.inc("r0"))
                v.wait_ge(*ch_g.at("t1", i))
                v.tensor_tensor(bneg[:, :, :], kkr[:, :, :], sig[:, 1, :, :], ALU.mult).then_inc(*c_.inc("kka"))
                v.wait_ge(*c_.at("kka", i))
                v.scalar_tensor_tensor(flat(bneg), flat(bneg), -1.0, flat(pinv), ALU.mult, ALU.mult).then_inc(
                    *c_.inc("bneg"))
                v.wait_ge(*ch_g.at("kp", i))
                v.tensor_tensor(flat(khat), flat(kp), flat(pinv), ALU.mult).then_inc(*c_.inc("khat"))
                v.wait_ge(*ch_pe.at("bon", i))
                v.tensor_tensor(bonv[:, :, :], ps[4][:, :].rearrange("p (m t) -> p m t", m=2),
                                rkv[2][:, ds(t0, 2), :], ALU.mult).then_inc(*c_.inc("bonv"))
                some(1)
                for p in range(2):
                    bank = ps[1 + p][:, :].rearrange("p (c u s) -> p c u s", c=CH, u=2)
                    v.wait_ge(*ch_pe.at(f"pb{p}", i))
                    if p == 0:
                        v.wait_ge(*ch_g.at("ui", i))
                    waited(v)
                    v.copy_predicated(ut[:, p, :, 0, :], level(0, 0, CH), bank[:, :, 0, :]).then_inc(*c_.inc(f"ub{p}"))
                    v.tensor_tensor(arb[:, p, :, :], bank[:, :, 1, :], mask(K_MBK + HD, CH), ALU.mult).then_inc(
                        *c_.inc(f"arb{p}"))
                    v.wait_ge(*ch_pe.at(f"pk{p}", i))
                    v.tensor_tensor(lka[:, p, :, :, :].rearrange("p c u s -> p c (u s)"),
                                    ps[3 + 2 * p][:, :].rearrange("p (c s) -> p c s", c=CH),
                                    con[:, K_MBK:K_MBK + P].unsqueeze(1).broadcast_to([P, CH, P]),
                                    ALU.mult).then_inc(*c_.inc(f"lk{p}"))
                v.wait_ge(*ch_pe.at("ln", i))
                v.tensor_tensor(lnm[:, :, :, :].rearrange("p a c s -> p (a c) s"),
                                ps[4][:, :].rearrange("p (c s) -> p c s", s=HD), mask(K_ML, 2 * CH),
                                ALU.mult).then_inc(*c_.inc("ln"))
                v.copy_predicated(ut[:, :, :, 1, :].rearrange("p a c s -> p (a c) s"), level(0, 1, 2 * CH),
                                  ps[4][:, :].rearrange("p (c s) -> p c s", s=HD)).then_inc(*c_.inc("tb"))
                for n in range(1, LEVELS):
                    for p in range(2):
                        v.wait_ge(*ch_pe.at(f"u{n}p{p}", i))
                        waited(v)
                        if n == LEVELS - 1:
                            v.copy_predicated(ut[:, p, :, 0, :], level(n, 0, CH),
                                              ps[2 + p][:, :].rearrange("p (c u s) -> p c u s", c=CH, u=2)[:, :, 0, :]
                                              ).then_inc(*c_.inc(f"u{n}p{p}"))
                        else:
                            v.copy_predicated(
                                ut[:, p, :, :, :].rearrange("p c u s -> p c (u s)"),
                                lvl[:, n, :].bitcast(I32).unsqueeze(1).broadcast_to([P, CH, P]),
                                ps[2 + p][:, :].rearrange("p (c s) -> p c s", c=CH)).then_inc(*c_.inc(f"u{n}p{p}"))
                    some(1)
                for c in range(CH):
                    v.wait_ge(*ch_pe.at(f"rhs{c}", i))
                    v.tensor_copy(rhs_s[:, :, :].rearrange("p a s -> p (a s)"), ps[4][:, 0:2 * HD]).then_inc(
                        *c_.inc(f"rhs{c}"))
                    if c == 0:
                        v.wait_ge(*ch_g.at("st", i))
                    for p in range(2):
                        v.tensor_scalar(std[:, p, :], st[:, c % 2, p, :], pcum[:, p, c, HD:HD + 1], None,
                                        ALU.mult).then_inc(*c_.inc(f"sp{c}" + "ab"[p]))
                    v.wait_ge(*ch_pe.at(f"sa{c}", i))
                    v.tensor_copy(sa[:, :, :].rearrange("p a s -> p (a s)"), ps[5][:, 0:2 * HD]).then_inc(
                        *c_.inc(f"sa{c}"))
                    v.wait_ge(*ch_pe.at(f"m{c}", i))
                    for p in range(2):
                        v.scalar_tensor_tensor(st[:, (c + 1) % 2, p, :], ps[6][:, p * HD:p * HD + HD],
                                               pcum[:, p, c, HD:HD + 1], std[:, p, :], ALU.mult, ALU.add).then_inc(
                                                   *c_.inc(f"st{c}" + "ab"[p]))
                    some((2, 3, 3, 2)[c])
                v.wait_ge(*ch_pe.at("mean", i))
                v.scalar_tensor_tensor(flat(yc), ps[1][:, :], -1.0 / HD, flat(ysb), ALU.mult, ALU.add).then_inc(
                    *c_.inc("yc"))
                v.wait_ge(*ch_a.at("sd", i))
                v.reciprocal(flat(nrm), flat(nrm)).then_inc(*c_.inc("rs"))
                v.wait_ge(*c_.at("rs", i))
                v.tensor_tensor(flat(yc), flat(yc), flat(nrm), ALU.mult).then_inc(*c_.inc("yn"))
                v.wait_ge(*c_.at("yn", i))
                for p in range(2):
                    v.tensor_scalar(yc[:, p, :], yc[:, p, :], col[:, ds(t0 + (C_GNW + p), 1)],
                                    col[:, ds(t0 + (C_GNB + p), 1)], ALU.mult, ALU.add).then_inc(*c_.inc(f"gn{p}"))
                v.wait_ge(*c_.at("gn1", i))
                v.tensor_tensor(flat(yc), flat(yc), flat(bonv), ALU.add).then_inc(*c_.inc("bo"))
                v.wait_ge(*c_.at("bo", i))
                v.tensor_tensor(flat(tmpa), flat(yc), flat(gate), ALU.mult).then_inc(*c_.inc("o"))
                adaln_out(ph_chunk, i)
                v.wait_ge(*ch_a.at("hi", i))
                v.tensor_tensor(act[:, ds(t0, 2), 1, :], tmpa[:, :, :], act[:, ds(t0, 2), 0, :].bitcast(F32),
                                ALU.subtract).then_inc(*c_.inc("lo"))
                assert m_[0] == KT, m_
            out_proj(2, ph_rwkv_out, 4)
            x_norm(3)
            up_proj(1)
            out_proj(3, ph_down[1], DOWN_PIECES)
            for n in range(8):
                v.wait_ge(*fin_pe.at(f"x{n}"))
                v.tensor_copy(xout[:, n // 4, (n % 4) * 512:(n % 4) * 512 + 512], ps[n % 4][:, :]).then_inc(
                    *fin_v.inc(f"x{n}"))

        @block.tensor
        def _(pe):
            def slab(ph, i, w0_, n, bank, src, kt0=0, tokens=False, ready=None):
                for q in range(n):
                    w = w0_ + q
                    half = ph.half(w)
                    pe.wait_ge(raw_done, ph.done(i, ph.w_at[w]))
                    if ready:
                        pe.wait_ge(*ready(q))
                    for k in range(PIECE_KT):
                        kt = kt0 + PIECE_KT * q + k
                        begin, end = q == 0 and k == 0, q == n - 1 and k == PIECE_KT - 1
                        for m in range(2):
                            for h, (w_, s_) in enumerate(((whi, 0), (whi, 1), (wlo, 0))):
                                if tokens:
                                    lhs, rhs = src[:, kt, s_, m * P:m * P + P], w_[:, half, k, :]
                                else:
                                    lhs, rhs = w_[:, half, k, m * P:m * P + P], src[:, kt, s_, :]
                                last = pe.matmul(ps[bank][:, m * S:m * S + S], lhs, rhs,
                                                 start=begin and m == 0 and h == 0, stop=end and h == 2,
                                                 skip_group_check=True)
                    last.then_inc(w_used, 1)

            def adaln_sum(ph, i, u=0):
                pe.wait_ge(raw_done, ph.done(i, ph.m_at[u * KT + KT - 1]))
                if not at_start(i, ph.unit0 + u):
                    pe.wait_ge(mod_written, ph.unit(i, u - 1))
                n = unit_cols[ph] // P
                for t in range(n):
                    last = pe.matmul(pmod[:, t:t + 1], mfin[:, t * P:t * P + P], ones[:, 0:1], start=True, stop=True,
                                     skip_group_check=True)
                last.then_inc(mod_summed, 1)

            def x_sum(n):
                s = norm[n]
                for t in range(KT):
                    if t % 4 == 0:
                        pe.wait_ge(*s["a"].at(f"sq{t // 4}"))
                    last = pe.matmul(ps[5][:, 0:S], ones, sq[:, t, :], start=t == 0, stop=t == KT - 1)
                last.then_inc(*s["pe"].inc("sum"))

            def out_proj(n, ph, per_slab, ready=None):
                o = outp[n]
                if ready:
                    pe.wait_ge(*ready)
                with pe.Fori(0, ph.iters) as i:
                    for s in range(4):
                        slab(ph, i, s * per_slab, per_slab, s, act)
                        if ph.units == 2 and s == 2:
                            adaln_sum(ph, i, 0)
                    if ph.units:
                        adaln_sum(ph, i, ph.units - 1)
                pe.wait_ge(*o["g"].at("add", NSLAB - 1))
                for m in range(2):
                    last = pe.matmul(ps[4][:, 0:S], ones, sqsum[:, m * S:m * S + S], start=m == 0, stop=m == 1)
                last.then_inc(*o["pe"].inc("sum"))

            pe.wait_ge(const_in, 16)
            pe.wait_ge(rows_in, 16 * (NROWS))
            for b, n in enumerate(ROW_COUNTS):
                last = pe.transpose(ps[b // 4][:, (b % 4) * P:(b % 4) * P + n], crow[0:n, b, :], ident[0:n, 0:n])
            last.then_inc(*se_pe.inc("rows"))
            pe.wait_ge(x_in, 16)
            for g in range(8):
                if g >= 3:
                    pe.wait_ge(*se_v.at(f"x{g - 3}"))
                for m in range(2):
                    for t in range(TT):
                        last = pe.transpose(ps[4 + g % 3][:, m * S + t * P:m * S + t * P + P],
                                            xtok[:, t, (2 * g + m) * P:(2 * g + m) * P + P], ident)
                last.then_inc(*se_pe.inc(f"x{g}"))
            adaln_sum(ph_mod, 0)
            with pe.Fori(1, 4) as i:
                adaln_sum(ph_mod, i)
            x_sum(0)

            def scores(a_):
                pe.wait_ge(*fx_a.at("k", a_))
                pe.wait_ge(*at_v.at("sel1", a_))
                for h in range(2):
                    for t in range(2):
                        dst = ps[3 + h][:, 0:P] if t == 0 else ps[3 + h][:, P:3 * P]
                        n = P * (t + 1)
                        pe.matmul(dst, qf[:, h, t * P:t * P + P], kf[:, h, 0:n], start=True, stop=False,
                                  skip_group_check=True)
                        last = pe.matmul(dst, ones[0:HEADS, :], nsel[:, h, 0:n], start=False, stop=True,
                                         skip_group_check=True)
                last.then_inc(*at_pe.inc("s"))

            def probs(a_):
                pe.wait_ge(*at_v.at("d11", a_))
                for h in range(2):
                    for b in range(3):
                        last = pe.matmul(ps[5 + h][:, b * P:b * P + P], ex[:, h, b * P:b * P + P],
                                         diag[:, h, min(b, 1), :], start=True, stop=True, skip_group_check=True)
                last.then_inc(*at_pe.inc("t"))

            def values(a_):
                pe.wait_ge(*at_v.at("p1", a_))
                pe.wait_ge(*fx_a.at("v", a_))
                for h in range(2):
                    pe.matmul(ps[3 + h][:, 0:S], vt_fox[:, 0, h * P:h * P + P], pt[:, h, 0:S], start=True, stop=False,
                              skip_group_check=True)
                    last = pe.matmul(ps[3 + h][:, P:S], vt_fox[:, 1, h * P:h * P + P], pt[:, h, S:3 * P],
                                     start=False, stop=True, skip_group_check=True)
                last.then_inc(*at_pe.inc("o"))

            def gate_logits():
                pe.wait_ge(*norm[0]["v"].at("lo3"))
                pe.wait_ge(*fg_v.at("lo"))
                for t in range(TT):
                    for kt in range(KT):
                        for h, (s_, w_) in enumerate(((0, wfh), (1, wfh), (0, wfl))):
                            pe.matmul(ps[3][:, t * HEADS:t * HEADS + HEADS], xs[:, kt, s_, t * P:t * P + P],
                                      w_[:, kt, :], start=kt == 0 and h == 0, stop=kt == KT - 1 and h == 2,
                                      skip_group_check=True)
                pe.matmul(ps[3][:, 32:32 + HEADS], ones[0:1, :], bf[0:1, :], start=True, stop=True,
                          skip_group_check=True).then_inc(*fg_pe.inc("z"))

            def gate_sums():
                pe.wait_ge(*fg_v.at("ls"))
                for t in range(TT):
                    last = pe.matmul(ps[3][0:HEADS, P:P + S], ga[:, t, :], triu[:, t, :], start=t == 0, stop=t == 1,
                                     skip_group_check=True)
                last.then_inc(*fg_pe.inc("cum"))

            def ready0(q):
                return norm[0]["v"].at(f"lo{q}")

            pe.wait_ge(fox_in, 64)
            slab(ph_fox, 0, 0, 4, 0, xs, ready=ready0)
            gate_logits()
            slab(ph_fox, 0, 4, 4, 1, xs)
            slab(ph_fox, 0, 8, 4, 2, xs, tokens=True)
            gate_sums()
            adaln_sum(ph_fox, 0)
            with pe.Fori(1, 8) as i:
                scores(i - 1)
                slab(ph_fox, i, 0, 4, 0, xs)
                probs(i - 1)
                slab(ph_fox, i, 4, 4, 1, xs)
                values(i - 1)
                slab(ph_fox, i, 8, 4, 2, xs, tokens=True)
                adaln_sum(ph_fox, i)
            scores(7)
            probs(7)
            values(7)
            out_proj(0, ph_fox_out, 4, at_v.at("lo1", 7))
            x_sum(1)

            def up_proj(n):
                with pe.Fori(0, UP_ITERS) as i:
                    slab(ph_up[n], i, 0, 4, 0, xs, ready=lambda q: norm[2 * n + 1]["v"].at(f"lo{q}"))
                    slab(ph_up[n], i, 4, 4, 1, xs)

            up_proj(0)
            out_proj(1, ph_down[0], DOWN_PIECES, up[0]["v2"].at("lo", UP_ITERS - 1))
            x_sum(2)

            for j, (w0_, nw_) in enumerate(((0, 2), (2, 2))):
                for q in range(nw_):
                    w = w0_ + q
                    pe.wait_ge(raw_done, ph_lora.done(0, w))
                    for r_ in (4 * j + 2 * q, 4 * j + 2 * q + 1):
                        pe.wait_ge(*mix_v.at("lo", r_))
                    for k in range(8):
                        kt = 8 * q + k
                        for h, (w_, s_) in enumerate(((whi, 0), (whi, 1), (wlo, 0))):
                            wk = w_[:, ph_lora.half(w), :, :].rearrange("p k n -> p (k n)")[:, k * LORA:(k + 1) * LORA]
                            last = pe.matmul(ps[4 + j][0:LORA, 0:S], wk, xs[:, kt, s_, :], start=kt == 0 and h == 0,
                                             stop=kt == KT - 1 and h == 2)
                    last.then_inc(w_used, 1)
            slab(ph_lora, 0, 4, 4, 6, xs, ready=lambda q: mix_v.at("lo", 8 + q))
            for j in range(3):
                with pe.Fori(0, 4) as i:
                    slab(ph_rkv[j], i, 0, 4, 0, xs, ready=lambda q: mix_v.at("lo", 4 * (3 + j) + q))
                    slab(ph_rkv[j], i, 4, 4, 1, xs)

            pe.wait_ge(*lo_a.at("tg"))
            heads = (slice(0, HD), slice(HD, P))

            def small_mm(dst, lhs, rhs, start=True, stop=True):
                return pe.matmul(dst, lhs, rhs, start=start, stop=stop, skip_group_check=True)

            with pe.Fori(0, ph_chunk.iters) as i:
                c_ = ch_pe
                pe.wait_ge(*ch_v.ended(i))
                pe.wait_ge(lw_in, i * 48 + 48)
                waited(pe)
                for p in range(2):
                    small_mm(ps[0][:, p * S:p * S + S], lw[0:LORA, 0, p * P:p * P + P], tw[:, :])
                    small_mm(ps[1][:, p * S:p * S + S], lw[0:LORA, 1, p * P:p * P + P], ta[:, :])
                    for k in range(2):
                        last = small_mm(ps[2][:, p * S:p * S + S], lw[:, 2 + k, p * P:p * P + P], tg[:, k, :],
                                        k == 0, k == 1)
                last.then_inc(*c_.inc("lora"))
                pe.wait_ge(*ch_g.at("sqk", i))
                waited(pe)
                for p in range(2):
                    last = small_mm(ps[3][:, p * S:p * S + S], blk, sqk[:, p, :])
                last.then_inc(*c_.inc("n2"))
                pe.wait_ge(*ch_g.at("rk1", i))
                waited(pe)
                for p in range(2):
                    last = small_mm(ps[4][:, p * S:p * S + S], blk, dec[:, p, :])
                last.then_inc(*c_.inc("bon"))

                def turn(name, bank, src, ready):
                    if ready:
                        pe.wait_ge(*ready)
                        waited(pe)
                    for p in range(2):
                        for c in range(CH):
                            for h in heads:
                                last_ = small_mm(bank[h, (p * CH + c) * HD:(p * CH + c + 1) * HD], src(h, p, c),
                                                 i64[h, :])
                    last_.then_inc(*c_.inc(name))

                turn("vtok", ps[5], lambda h, p, c: vloc[h, p, c * HD:(c + 1) * HD], ch_g.at("v", i))
                turn("btok", ps[6], lambda h, p, c: bneg[h, p, c * HD:(c + 1) * HD], ch_v.at("bneg", i))
                pe.wait_ge(*ch_a.at("sw1", i))
                waited(pe)
                turn("ktok", ps[0], lambda h, p, c: khat[h, p, c * HD:(c + 1) * HD], ch_v.at("khat", i))
                for p in range(2):
                    pe.wait_ge(*ch_a.at("gate", i))
                    waited(pe)
                    for c in range(CH):
                        for h in heads:
                            last = small_mm(ps[1 + p][h, c * P:c * P + P], bneg[h, p, c * HD:(c + 1) * HD],
                                            rr[h, p, c, :, :].rearrange("p u s -> p (u s)"))
                    last.then_inc(*c_.inc(f"pb{p}"))
                    pe.wait_ge(*ch_a.at("nrm" if p == 0 else "vt", i))
                    waited(pe)
                    for c in range(CH):
                        for h in heads:
                            last = small_mm(ps[3 + 2 * p][h, c * P:c * P + P], khat[h, p, c * HD:(c + 1) * HD],
                                            rr[h, p, c, :, :].rearrange("p u s -> p (u s)"))
                    last.then_inc(*c_.inc(f"pk{p}"))
                pe.wait_ge(*ch_v.at("bonv", i))
                waited(pe)
                for p in range(2):
                    for c in range(CH):
                        for h in heads:
                            last = small_mm(ps[4][h, (p * CH + c) * HD:(p * CH + c + 1) * HD], rr[h, p, c, 0, :],
                                            bneg[h, p, c * HD:(c + 1) * HD])
                last.then_inc(*c_.inc("ln"))
                pe.wait_ge(*ch_a.at("kt", i))
                waited(pe)
                for n in range(1, LEVELS):
                    for p in range(2):
                        if n == 1:
                            pe.wait_ge(*ch_v.at("tb", i))
                            waited(pe)
                        else:
                            pe.wait_ge(*ch_v.at(f"u{n - 1}p{p}", i))
                            waited(pe)
                        for c in range(CH):
                            for h in heads:
                                last = small_mm(ps[p][h, c * HD:(c + 1) * HD], lnm[h, p, c, :], ut[h, p, c, 0, :])
                        last.then_inc(*c_.inc(f"z{n}p{p}"))
                    for p in range(2):
                        pe.wait_ge(*ch_a.at(f"z{n}p{p}", i))
                        waited(pe)
                        for c in range(CH):
                            for h in heads:
                                last = small_mm(ps[2 + p][h, c * P:c * P + HD], ut[h, p, c, 1, :], zsb[h, p, c, :])
                                if n < LEVELS - 1:
                                    last = small_mm(ps[2 + p][h, c * P + HD:(c + 1) * P], zsb[h, p, c, :],
                                                    ut[h, p, c, 1, :])
                        last.then_inc(*c_.inc(f"u{n}p{p}"))
                pe.wait_ge(*ch_v.at(f"u{LEVELS - 1}p1", i))
                waited(pe)
                for c in range(CH):
                    if c:
                        pe.wait_ge(*ch_v.at(f"st{c - 1}b", i))
                        waited(pe)
                    else:
                        pe.wait_ge(*ch_g.at("st", i))
                        waited(pe)
                    for p in range(2):
                        for h in heads:
                            small_mm(ps[4][h, p * HD:p * HD + HD], rr[h, p, c, 0, :], st[h, c % 2, p, :], True, False)
                            last = small_mm(ps[4][h, p * HD:p * HD + HD], lka[h, p, c, 0, :], vtok[h, p, c, :],
                                            False, True)
                    last.then_inc(*c_.inc(f"rhs{c}"))
                    pe.wait_ge(*ch_v.at(f"rhs{c}", i))
                    waited(pe)
                    for p in range(2):
                        for h in heads:
                            last = small_mm(ps[5][h, p * HD:p * HD + HD], ut[h, p, c, 0, :], rhs_s[h, p, :])
                    last.then_inc(*c_.inc(f"sa{c}"))
                    pe.wait_ge(*ch_v.at(f"sa{c}", i))
                    waited(pe)
                    for p in range(2):
                        for h in heads:
                            small_mm(ps[6][h, p * HD:p * HD + HD], btok[h, p, c, :], sa[h, p, :], True, False)
                            last = small_mm(ps[6][h, p * HD:p * HD + HD], ktok[h, p, c, :], vtok[h, p, c, :],
                                            False, True)
                    last.then_inc(*c_.inc(f"m{c}"))
                    for p in range(2):
                        for h in heads:
                            dst = ps[0][h, (p * CH + c) * HD:(p * CH + c + 1) * HD]
                            small_mm(dst, st[h, c % 2, p, :], rr[h, p, c, 1, :], True, False)
                            small_mm(dst, vtok[h, p, c, :], lka[h, p, c, 1, :], False, False)
                            last = small_mm(dst, sa[h, p, :], arb[h, p, c, :], False, True)
                    last.then_inc(*c_.inc(f"y{c}"))
                adaln_sum(ph_chunk, i)
                pe.wait_ge(*ch_a.at("y", i))
                for p in range(2):
                    last = small_mm(ps[1][:, p * S:p * S + S], blk, ysb[:, p, :])
                last.then_inc(*c_.inc("mean"))
                pe.wait_ge(*ch_a.at("sqy", i))
                for p in range(2):
                    last = small_mm(ps[2][:, p * S:p * S + S], blk, sqk[:, p, :])
                last.then_inc(*c_.inc("var"))
            out_proj(2, ph_rwkv_out, 4, ch_v.ended(8))
            x_sum(3)
            up_proj(1)
            out_proj(3, ph_down[1], DOWN_PIECES, up[1]["v2"].at("lo", UP_ITERS - 1))
            for n in range(8):
                pe.wait_ge(*outp[3]["v"].at(f"x{n % 4}"))
                if n >= 4:
                    pe.wait_ge(*fin_v.at(f"x{n - 4}"))
                for q in range(4):
                    t = 4 * (n % 4) + q
                    last = pe.transpose(ps[n % 4][:, q * P:q * P + P], x[:, t, (n // 4) * P:(n // 4) * P + P], ident)
                last.then_inc(*fin_pe.inc(f"x{n}"))


_INS = ["x", "c", "mod_w", "mod_b", "norm_g", "fox_w_in", "fox_b_f", "fox_w_out", "rwkv_mu", "rwkv_w0", "rwkv_w1",
        "rwkv_w2", "rwkv_a0", "rwkv_a1", "rwkv_a2", "rwkv_g1", "rwkv_g2", "rwkv_k_k", "rwkv_k_a", "rwkv_r_k",
        "rwkv_w_r", "rwkv_w_k", "rwkv_w_v", "rwkv_w_o", "rwkv_gn_w", "rwkv_gn_b", "ffn_w_in", "ffn_conv_w",
        "ffn_conv_b", "ffn_w_out"]


def kernel(**inputs):
    import concourse.bacc as _bacc
    from concourse.bass_utils import run_bass_kernel_spmd as _run

    nc = _bacc.Bacc("TRN2", target_bir_lowering=False, num_devices=1)
    arrays, aps = {}, {}
    for name in _INS + ["consts"]:
        array = shape_constants() if name == "consts" else np.ascontiguousarray(inputs[name])
        arrays[f"in_{name}"] = array
        aps[name] = nc.dram_tensor(f"in_{name}", array.shape, F32, kind="ExternalInput").ap()
    out = nc.dram_tensor("out", (1, S, D), F32, kind="ExternalOutput").ap()
    trunk(nc, aps, out)
    r = _run(nc, [arrays], core_ids=[0])
    return r.results[0]["out"]
```

```python
import math
from contextlib import ExitStack

import numpy as np

import concourse.bass as bass
from concourse import mybir

F32 = mybir.dt.float32
F32R = mybir.dt.float32r
I32 = mybir.dt.int32
ALU = mybir.AluOpType
ACT = mybir.ActivationFunctionType
AX_X = mybir.AxisListType.X
ds = bass.ds

P = 128
D = 2048
S = 256
FF = 5632
KT = D // P
FT = FF // P
TT = S // P
SLAB = 256
NSLAB = D // SLAB
HEADS = 16
LORA = 96
HD = 64
CH = S // HD
NR, NH = 4, 4
PIECE_KT = 4
NORM_EPS, GN_EPS = 1e-6, 64e-5
DECAY_RATE = -math.exp(-0.5)
UP_ITERS = FF // SLAB
DOWN_PIECES = FT // PIECE_KT

C_COND, C_W0, C_A0, C_KK, C_KA, C_RK, C_GNW, C_GNB = range(0, 128, 16)
C_NORM = 128
C_MODB = 256
C_MU = 448
C_CONVW = 544
C_CONVB = C_CONVW + 6 * 2 * FT
C_ALL = C_CONVB + 2 * 2 * FT
MODT = 96

K_ID, K_ONE, K_BLK, K_I64, K_MBK, K_ML, K_EPS = 0, 128, 256, 384, 448, 576, 640
K_MAIN = 644
K_CAUSAL, K_TRIU = K_MAIN, K_MAIN + 384
K_LEVEL = K_TRIU + 512
K_ALL = K_LEVEL + 6 * 128
ROW_COUNTS = [P, P, MODT, MODT, 6 * KT] + [2 * FT] * 8
LEVELS = 6


def shape_constants():
    k = np.zeros((P, K_ALL), np.float32)
    p = np.arange(P)[:, None]
    j = np.arange(P)[None, :]
    h, q = p % HD, np.arange(HD)[None, :]
    k[:, K_ID:K_ID + P] = p == j
    k[:, K_ONE:K_ONE + P] = 1.0
    k[:, K_BLK:K_BLK + P] = p // HD == j // HD
    k[:, K_I64:K_I64 + HD] = h == q
    k[:, K_MBK:K_MBK + HD] = h < q
    k[:, K_MBK + HD:K_MBK + 2 * HD] = h <= q
    k[:, K_ML:K_ML + HD] = q < h
    k[:, K_EPS], k[:, K_EPS + 1] = NORM_EPS, GN_EPS
    k[:, K_CAUSAL:K_CAUSAL + P] = np.where(j <= p, 0.0, -1e30)
    k[:, K_CAUSAL + 2 * P:K_CAUSAL + 3 * P] = np.where(j <= p, 0.0, -1e30)
    t = np.arange(S)[None, :]
    for tile in range(TT):
        k[:, K_TRIU + tile * S:K_TRIU + (tile + 1) * S] = p + tile * P <= t
    for n in range(LEVELS):
        m = 1 << n
        lower = (h // m == q // m + 1) & ((q // m) % 2 == 0)
        upper = (q // m == h // m + 1) & ((h // m) % 2 == 0)
        k[:, K_LEVEL + n * P:K_LEVEL + n * P + HD] = upper
        k[:, K_LEVEL + n * P + HD:K_LEVEL + (n + 1) * P] = lower
    return k


class Phase:
    raw_count = weight_count = unit_count = 0
    ring_count = [0, 0]
    holder = {}

    def __init__(self, iters, pattern, early=0):
        assert pattern[:early] == "W" * early and early <= NH
        self.early = early
        assert pattern.count("W") % NH == 0 and (len(pattern) - pattern.count("W")) % KT == 0
        self.iters, self.pattern = iters, pattern
        self.raw0, self.w0, self.unit0 = Phase.raw_count, Phase.weight_count, Phase.unit_count
        self.ring0, self.held = list(Phase.ring_count), dict(Phase.holder)
        self.nw, self.units = pattern.count("W"), (len(pattern) - pattern.count("W")) // KT
        self.w_at = [k for k, c in enumerate(pattern) if c == "W"]
        self.m_at = [k for k, c in enumerate(pattern) if c != "W"]
        self.rings = [[k for k, c in enumerate(pattern) if (c == "M") == bool(ring)] for ring in range(2)]
        self.place = {k: (ring, n) for ring in range(2) for n, k in enumerate(self.rings[ring])}
        assert all(len(ring) % NR == 0 for ring in self.rings)
        Phase.raw_count += iters * len(pattern)
        Phase.weight_count += iters * self.nw
        Phase.unit_count += iters * self.units
        for ring in range(2):
            Phase.ring_count[ring] += iters * len(self.rings[ring])
            for k in self.rings[ring][-NR:]:
                Phase.holder[self.raw(k)] = self.done(iters - 1, k)

    def raw(self, k):
        ring, n = self.place[k]
        return ring * NR + (self.ring0[ring] + n) % NR

    def landed(self, i, k):
        ring, n = self.place[k]
        return i * (16 * len(self.rings[ring]) // NR) + 16 * ((self.ring0[ring] + n) // NR + 1)

    def done(self, i, k):
        return i * len(self.pattern) + (self.raw0 + k + 1)

    def freed(self, i, k):
        ring, n = self.place[k]
        if n >= NR:
            return self.done(i, self.rings[ring][n - NR])
        if at_start(i, 0):
            return self.held.get(self.raw(k), 0)
        return self.done(i, self.rings[ring][n - NR]) - len(self.pattern)

    def half(self, w):
        return (self.w0 + w) % NH

    def weight(self, i, w):
        return i * self.nw + (self.w0 + w + 1)

    def unit(self, i, u=0):
        return i * self.units + (self.unit0 + u + 1)


class Steps:

    def __init__(self, sem, names, first=""):
        self.sem, self.names, self.first, self.next = sem, names.split(), first.split(), 0
        assert len(set(self.names + self.first)) == len(self.names + self.first), names

    def inc(self, name):
        n = self.next - len(self.first)
        due = self.first[self.next] if n < 0 else self.names[n % len(self.names)]
        assert due == name, (due, name)
        self.next += 1
        return self.sem, 1

    def at(self, name, i=0):
        if name in self.first:
            return self.sem, self.first.index(name) + 1
        return self.sem, i * len(self.names) + (len(self.first) + self.names.index(name) + 1)

    def ended(self, i):
        assert self.first
        return self.sem, i * len(self.names) + len(self.first)


def at_start(i, n):
    return isinstance(i, int) and i == 0 and n <= 0


def spread(w, m, kind="m"):
    out, given = "", 0
    for n in range(w):
        out += "W"
        while given < m * (n + 1) // w:
            out, given = out + kind, given + 1
    return out


def trunk(nc, a, out):
    Phase.raw_count = Phase.weight_count = Phase.unit_count = 0
    Phase.ring_count, Phase.holder = [0, 0], {}
    ph_mod = Phase(4, "Mm" * (KT // 2))
    ph_fox = Phase(8, "WW" + spread(10, KT, "M"), early=2)
    ph_fox_out = Phase(2, "WWWW" + spread(12, KT, "M"), early=4)
    ph_up = [None, None]
    ph_down = [None, None]
    ph_up[0] = Phase(UP_ITERS, "W" * 8, early=4)
    ph_down[0] = Phase(2, "WWWW" + spread(4 * DOWN_PIECES - 4, 2 * KT), early=4)
    ph_lora = Phase(1, "W" * 8, early=4)
    ph_rkv = [Phase(4, "W" * 8) for _ in range(3)]
    ph_chunk = Phase(8, "m" * KT)
    ph_rwkv_out = Phase(2, "W" * 16)
    ph_up[1] = Phase(UP_ITERS, "W" * 8, early=4)
    ph_down[1] = Phase(2, "W" * (4 * DOWN_PIECES), early=4)
    unit_cols = {ph_mod: 1024, ph_fox: 768, ph_fox_out: 1024, ph_down[0]: 1024, ph_chunk: 1024}
    unit_tile0 = {ph_mod: 0, ph_fox: 32, ph_fox_out: 80, ph_down[0]: MODT, ph_chunk: MODT + 32}

    ctx = ExitStack()
    with ctx:
        nsem = [0]

        def sem(name):
            nsem[0] += 1
            return ctx.enter_context(nc.semaphore(name))

        top = nc.sbuf_usable_end
        base = (nc.sbuf_base + 31) // 32 * 32
        O_X = base
        O_XS = O_X + 4 * KT * S
        O_RAW = O_XS + 8 * KT * S
        O_HI = O_RAW + NR * 4096
        O_LO = O_HI + NH * 4096
        O_ACT = O_LO + NH * 4096
        O_SMALL = O_ACT + 8 * FT * S

        def at(name, offset, shape, dt=F32):
            n = 4
            for s in shape[1:]:
                n *= s
            return nc.alloc_sbuf_tensor_at(name, shape, dt, offset=offset), offset + n

        def take(region, name, shape, dt=F32):
            region[0] = (region[0] + 31) // 32 * 32
            t, region[0] = at(name, region[0], shape, dt)
            assert region[0] <= region[1], (name, region)
            return t

        x, _ = at("x", O_X, [P, KT, S])
        xs, _ = at("xs", O_XS, [P, KT, 2, S], F32R)
        y, _ = at("y", O_XS, [P, KT, S])
        sq, _ = at("sq", O_XS + 4 * KT * S, [P, KT, S])
        raw, _ = at("raw", O_RAW, [P, NR, 1024])
        whi, _ = at("whi", O_HI, [P, NH, 4, SLAB], F32R)
        wlo, _ = at("wlo", O_LO, [P, NH, 4, SLAB], F32R)
        act, _ = at("act", O_ACT, [P, FT, 2, S], F32R)
        small = [O_SMALL, top]
        col = take(small, "col", [P, C_ALL])
        con = take(small, "con", [P, K_MAIN])
        mod = take(small, "mod", [P, 2 * MODT])
        cact = take(small, "cact", [P, KT])
        cexp = take(small, "cexp", [P, KT])
        ncol = take(small, "ncol", [P, KT])
        omu = take(small, "omu", [P, 6 * KT])
        pcol = take(small, "pcol", [P, 4, 2])
        gain_in = take(small, "gain_in", [P, KT])
        gain_out = take(small, "gain_out", [P, KT])
        rs = take(small, "rs", [P, S])
        sqsum = take(small, "sqsum", [P, 2 * S])
        o_macc = small[0] = (small[0] + 31) // 32 * 32
        macc = take(small, "macc", [P, 1024])
        mfin = take(small, "mfin", [P, 1024])
        fend = small[0]
        ub, e = at("ub", o_macc, [P, 4, S + 2])
        tb4, _ = at("tb4", o_macc, [P, 4, S])
        vb, e = at("vb", (e + 31) // 32 * 32, [P, 4, S])
        small[0] = max(small[0], e)

        r = [O_ACT, O_SMALL]
        xtok = take(r, "xtok", [P, TT, D])
        crow = take(r, "crow", [P, 13, P])
        r = [O_ACT + 8 * KT * S, O_SMALL]
        wf = take(r, "wf", [P, KT, HEADS])
        wfh = take(r, "wfh", [P, KT, HEADS], F32R)
        wfl = take(r, "wfl", [P, KT, HEADS], F32R)
        bf = take(r, "bf", [1, HEADS])
        gz = take(r, "gz", [P, TT, HEADS])
        ga = take(r, "ga", [P, TT, HEADS])
        gb = take(r, "gb", [P, TT, HEADS])
        gbf = take(r, "gbf", [P, HEADS])
        triu = take(r, "triu", [P, TT, S])
        causal = take(r, "causal", [P, 3 * P])
        negc = take(r, "negc", [HEADS, S])
        nsel = take(r, "nsel", [HEADS, 2, S])
        qf = take(r, "qf", [P, 2, S])
        kf = take(r, "kf", [P, 2, S])
        vt_fox = take(r, "vt_fox", [P, TT, SLAB])
        sm = take(r, "sm", [P, 2, 3 * P])
        ex = take(r, "ex", [P, 2, 3 * P])
        pt = take(r, "pt", [P, 2, 3 * P])
        nmax = take(r, "nmax", [P, 2, 2])
        den = take(r, "den", [P, 2, 2])
        dinv = take(r, "dinv", [P, 2, 2])
        diag = take(r, "diag", [P, 2, 2, P])
        raw2 = take(r, "raw2", [P, NR, 1024])
        slots = [raw[:, n, :] for n in range(NR)] + [raw2[:, n, :] for n in range(NR)]
        rk, _ = at("rk", O_ACT, [P, KT, 2, S])
        O_V = O_ACT + 8 * KT * S
        O_HB = O_V + 8 * KT * S
        vfm, _ = at("vfm", O_V, [P, KT, S])
        r = [O_HB, O_SMALL]
        hb = take(r, "hb", [P, KT, S + 1])
        o_hb_end = r[0]
        lvl = take(r, "lvl", [P, LEVELS, P])
        tw = take(r, "tw", [LORA, S])
        ta = take(r, "ta", [LORA, S])
        tg = take(r, "tg", [P, 2, S])
        mx, e = at("mx", o_macc, [P, 4, 2, S])
        assert e <= fend, (e, fend)
        xsb, _ = at("xsb", O_V, [P, KT, 2, S], F32R)
        r1 = [O_XS, O_RAW]
        r2 = [O_HI, O_ACT]
        r3 = [O_V + 4 * KT * S, o_hb_end]
        U = [P, 2, S]
        sig = take(r1, "sig", [P, 2, 2, S])
        dec = take(r1, "dec", U)
        kkr = take(r1, "kkr", U)
        sqk = take(r1, "sqk", U)
        nrm = take(r1, "nrm", U)
        tmpa = take(r1, "tmpa", U)
        kp = take(r1, "kp", U)
        pinv = take(r1, "pinv", U)
        bneg = take(r1, "bneg", U)
        zsb = take(r1, "zsb", [P, 2, CH, HD])
        lnm = take(r1, "lnm", [P, 2, CH, HD])
        pcum = take(r1, "pcum", [P, 2, CH, HD + 1])
        zero = take(small, "zero", [P, HD])
        khat, vloc = pinv, tmpa
        rr = [take(r2, f"rr{q}", [P, 2, CH, 2, HD]) for q in range(2)]
        lka = [take(r2, f"lka{q}", [P, 2, CH, 2, HD]) for q in range(2)]
        ut = [take(r2, f"ut{q}", [P, 2, CH, 2, HD]) for q in range(2)]
        gate = [take(r2, f"gate{q}", U) for q in range(2)]
        bonv = [take(r2, f"bonv{q}", U) for q in range(2)]
        vtok = [take(r3, f"vtok{q}", [P, 2, CH, HD]) for q in range(2)]
        btok = [take(r3, f"btok{q}", [P, 2, CH, HD]) for q in range(2)]
        ktok = [take(r3, f"ktok{q}", [P, 2, CH, HD]) for q in range(2)]
        arb = [take(r3, f"arb{q}", [P, 2, CH, HD]) for q in range(2)]
        lw = take(r3, "lw", [P, 4, SLAB])
        nry = take(r3, "nry", U)
        yc = take(r3, "yc", U)
        sqy = take(r3, "sqy", U)
        ysb = take(r3, "ysb", U)
        pend = [take(small, f"pend{q}", [P, 2, CH]) for q in range(2)]
        st = take(r1, "st", [P, 2, 2, HD])
        std = take(r1, "std", [P, 2, HD])
        rhs_s = take(small, "rhs_s", [P, 2, HD])
        sa = take(small, "sa", [P, 2, HD])
        r = [O_ACT, O_SMALL]
        xout = take(r, "xout", [P, TT, D])

        ps = [ctx.enter_context(nc.psum_tensor(f"ps{b}", [P, 512], F32)) for b in range(8)]
        pmod = ps[7]

        ident, ones, blk = (con[:, k:k + P] for k in (K_ID, K_ONE, K_BLK))
        i64 = con[:, K_I64:K_I64 + HD]
        eps = [con[:, K_EPS:K_EPS + 1], con[:, K_EPS + 1:K_EPS + 2]]

        raw_in = [sem(f"raw_in{n}") for n in range(2 * NR)]
        raw_done = sem("raw_done")
        w_hi = sem("w_hi")
        w_used = sem("w_used")
        mod_summed = sem("mod_summed")
        mod_written = sem("mod_written")
        const_in, rows_in, x_in, fox_in, lvl_in, lw_in, out_done = (
            sem(n) for n in ("const_in", "rows_in", "x_in", "fox_in", "lvl_in", "lw_in", "out_done"))
        NROWS = 20

        def steps(name, names, first=""):
            return Steps(sem(name), names, first)

        groups = range(4)
        se_pe = steps("se_pe", "rows x0 x1 x2 x3 x4 x5 x6 x7")
        se_v = steps("se_v", "cols ncol omu csum ce cact x0 x1 x2 x3 x4 x5 x6 x7")
        se_a = steps("se_a", "cexp")
        norm = [dict(v=steps(f"norm{n}_v", "rinv gain " + ("t0 t1 t2 t3" if n == 2 else "t0 t1 lo0 t2 lo1 t3 lo2 lo3")),
                     a=steps(f"norm{n}_a", "sq0 sq1 sq2 sq3 root hi0 hi1 hi2 hi3"),
                     pe=steps(f"norm{n}_pe", "sum")) for n in range(4)]
        outp = [dict(a=steps(f"out{n}_a", "y sq"), g=steps(f"out{n}_g", "add"),
                     pe=steps(f"out{n}_pe", "sum"), root=steps(f"out{n}_root", "root"),
                     v=steps(f"out{n}_v", "gain rinv " + " ".join(f"t{g} x{g}" for g in groups)))
                for n in range(4)]
        fg_pe = steps("fg_pe", "z cum")
        fg_a = steps("fg_a", "hi e l")
        fg_v = steps("fg_v", "lo b z abs min ls neg")
        fx_a = steps("fx_a", "q k v")
        at_pe = steps("at_pe", "s t o")
        at_v = steps("at_v", "sel0 sel1 sm0 sm1 m00 m01 m10 m11 rd d00 d01 d10 d11 p0 p1 lo0 lo1")
        at_a = steps("at_a", "e00 e01 e10 e11 hi0 hi1")
        up = [dict(a1=steps(f"up{n}_a1", "u t0 t1 g"), a2=steps(f"up{n}_a2", "u t0 t1 hi"),
                   v1=steps(f"up{n}_v1", "p0 p1 c0 c1"), v2=steps(f"up{n}_v2", "p0 p1 c0 c1 prod lo"),
                   z=steps(f"up{n}_z", "zero")) for n in range(2)]
        lo_a = steps("lo_a", "tw ta tg")
        mix_zero = steps("mix_zero", "zero")
        mix_now, mix_sum, mix_hi, mix_lo = (steps(f"mix_{n}", n) for n in ("now", "sum", "hi", "lo"))
        rk_a = [steps(f"rk_a{n}", "s0 s1") for n in range(3)]
        hd_pe = steps("hd_pe", "lora n2 bon")
        hd_a = steps("hd_a", "sw0 sw1 sa0 sa1 dec gate nrm")
        hd_v = steps("hd_v", " ".join(f"p{n}" for n in range(8)) + " pend nmx nrc kkn r0 pinv r1 bonv kka bneg khat")
        hd_g = steps("hd_g", "c0 c1 c2 c3 k kk0 kk1 sqk t0 t1 kp rk rk0 rk1 v ui")
        pr_pe = steps("pr_pe", "vtok btok ktok pb0 pk0 pb1 pk1 ln "
                      + " ".join(f"z{n}p0 z{n}p1 u{n}p0 u{n}p1" for n in range(1, LEVELS)))
        pr_a = steps("pr_a", "vt bt kt " + " ".join(f"z{n}p{p}" for n in range(1, LEVELS) for p in range(2)))
        pr_v = steps("pr_v", "ub0 arb0 lk0 ub1 arb1 lk1 ln tb "
                     + " ".join(f"u{n}p{p}" for n in range(1, LEVELS) for p in range(2)), "zero pone")
        sc_pe = steps("sc_pe", " ".join(f"rhs{c} sa{c} m{c} y{c}" for c in range(CH)) + " mean var")
        sc_a = steps("sc_a", " ".join(f"rhs{c} sa{c}" for c in range(CH)) + " y sqy sd hi")
        sc_v = steps("sc_v", "z " + " ".join(f"sp{c}a sp{c}b st{c}a st{c}b" for c in range(CH))
                     + " yc rs yn gn0 gn1 bo o lo", "first")
        fin_pe = steps("fin_pe", " ".join(f"x{n}" for n in range(8)))
        fin_v = steps("fin_v", " ".join(f"x{n}" for n in range(8)))

        def feat(w):
            return w.rearrange("(k p) n -> p k n", p=P)

        mod_w = [feat(a["mod_w"][n]) for n in range(2)]
        fox_w_in, fox_w_out = feat(a["fox_w_in"][0]), feat(a["fox_w_out"][0])
        w_rkv = [feat(a[n][0]) for n in ("rwkv_w_r", "rwkv_w_k", "rwkv_w_v")]
        w_o = feat(a["rwkv_w_o"][0])
        w_up = [feat(a["ffn_w_in"][n]) for n in range(2)]
        w_down = [feat(a["ffn_w_out"][n]) for n in range(2)]
        w1, a1, g1 = (feat(a[n][0]) for n in ("rwkv_w1", "rwkv_a1", "rwkv_g1"))

        def rows(ap):
            return ap.rearrange("(t p) -> t p", p=P)

        def flat(t):
            return t[:, :, :].rearrange("p a s -> p (a s)")

        def chunks(t):
            return flat(t).rearrange("p (c s) -> p c s", s=HD)

        def chunks_at(t, tile):
            return t[:, ds(tile, 2), :].rearrange("p a (c s) -> p (a c) s", s=HD)

        def pairs(t):
            return t[:, :, :, :].rearrange("p a c s -> p (a c) s")

        def mask(k, n):
            return con[:, k:k + HD].unsqueeze(1).broadcast_to([P, n, HD])

        def level(n, u, copies):
            return lvl[:, n, u * HD:(u + 1) * HD].bitcast(I32).unsqueeze(1).broadcast_to([P, copies, HD])

        def level_blocks(n, copies):
            return lvlb[:, n, :].bitcast(I32).rearrange("p (h s) -> p h s", h=2).unsqueeze(1).broadcast_to(
                [P, copies, 2, HD])

        MIXES = (1, 4, 5, 0, 2, 3)

        def mix_to(m):
            return xs if m % 2 else xsb

        def mix_free(m):
            return (ph_lora.weight(0, 1), ph_lora.weight(0, 3), ph_lora.weight(0, 7), ph_rkv[0].weight(3, 7))[m - 2]

        def shift_col(n, t):
            k = MODT * (n // 2) + 3 * KT * (n % 2) + t
            return mod[:, k:k + 1]

        def waited(engine):
            engine.nop(nofuse=True)

        heads = (slice(0, HD), slice(HD, P))

        def chunk_laps(engine, head, lap):
            n = ph_chunk.iters
            head(0, 0)
            lap(0, 0, turn=False)
            with engine.Fori(0, n // 2 - 1) as j:
                lap(j * 2 + 1, 1)
                lap(j * 2 + 2, 0)
            lap(n - 1, 1, ahead=False)
            lap(n, 0, prep=False, ahead=False)

        block = ctx.enter_context(nc.Block())

        @block.sync
        def _(sp):
            def piece(ph, i, k, src, n=None):
                slot = ph.raw(k)
                free = ph.freed(i, k)
                if not isinstance(free, int) or free > 0:
                    sp.wait_ge(raw_done, free)
                dst = slots[slot] if n is None else slots[slot][:, 0:n]
                if len(src.shape) == 3 and src.shape[1] > 1:
                    dst = dst.rearrange("p (k n) -> p k n", k=src.shape[1])
                elif len(src.shape) == 3:
                    dst = dst.rearrange("p (k n) -> p k n", k=1)
                sp.dma_start(dst, src).then_inc(raw_in[slot], 16)

            def stream(ph, i, wsrc, layer=0, tile0=0):
                w = m = 0
                cols = unit_cols.get(ph, 0)
                for k, c in enumerate(ph.pattern):
                    if c == "W":
                        piece(ph, i, k, wsrc(w))
                        w += 1
                    else:
                        u, kt = divmod(m, KT)
                        at_col = i * (cols * ph.units) + (tile0 * P + u * cols)
                        piece(ph, i, k, mod_w[layer][:, kt:kt + 1, ds(at_col, cols)], cols)
                        m += 1

            def laps(n, body):
                body(0)
                with sp.Fori(1, n) as i:
                    body(i)

            sp.dma_start(con[:, :], a["consts"][:, 0:K_MAIN]).then_inc(const_in, 16)
            def mod_piece(i, k):
                piece(ph_mod, i, k, mod_w[0][:, k:k + 1, ds(i * 1024, 1024)], 1024)

            for k in range(KT):
                mod_piece(0, k)
            with sp.Fori(1, ph_mod.iters) as i:
                for k in range(KT):
                    mod_piece(i, k)
            def fox_pieces(i):
                stream(ph_fox, i, lambda w: fox_w_in[:, 4 * (w % 4):4 * (w % 4) + 4,
                                                     ds(i * SLAB + (w // 4) * D, SLAB)], 0, 32)

            laps(ph_fox.iters, fox_pieces)

            def out_pieces(ph, wt, per_slab, layer=0, tile0=0):
                def one(i):
                    stream(ph, i, lambda w: wt[:, 4 * (w % per_slab):4 * (w % per_slab) + 4,
                                               ds(i * (4 * SLAB) + (w // per_slab) * SLAB, SLAB)], layer, tile0)

                laps(ph.iters, one)

            def up_pieces(n):
                def one(i):
                    stream(ph_up[n], i, lambda w: w_up[n][:, 4 * (w % 4):4 * (w % 4) + 4,
                                                          ds(i * SLAB + (w // 4) * FF, SLAB)])

                laps(UP_ITERS, one)

            out_pieces(ph_fox_out, fox_w_out, 4, 0, 80)
            up_pieces(0)
            out_pieces(ph_down[0], w_down[0], DOWN_PIECES, 1, 0)
            for k in range(2):
                piece(ph_lora, 0, k, w1[:, 8 * k:8 * k + 8, :], 8 * LORA)
            for k in range(2):
                piece(ph_lora, 0, 2 + k, a1[:, 8 * k:8 * k + 8, :], 8 * LORA)
            for k in range(4):
                piece(ph_lora, 0, 4 + k, g1[:, 4 * k:4 * k + 4, :])
            for j in range(3):
                with sp.Fori(0, 4) as i:
                    stream(ph_rkv[j], i, lambda w: w_rkv[j][:, 4 * (w % 4):4 * (w % 4) + 4,
                                                            ds(i * (2 * SLAB) + (w // 4) * SLAB, SLAB)])
            sp.wait_ge(*norm[2]["a"].at("hi3"))
            sp.dma_start(lvl[:, :, :], a["consts"][:, K_LEVEL:K_LEVEL + LEVELS * P].rearrange(
                "p (l s) -> p l s", l=LEVELS)).then_inc(lvl_in, 16)

            def lora_second(i):
                sp.dma_start(lw[0:LORA, 0, :], a["rwkv_w2"][0][:, ds(i * SLAB, SLAB)]).then_inc(lw_in, 16)
                sp.dma_start(lw[0:LORA, 1, :], a["rwkv_a2"][0][:, ds(i * SLAB, SLAB)]).then_inc(lw_in, 16)
                sp.dma_start(lw[:, 2:4, :], a["rwkv_g2"][0].rearrange("(k p) n -> p k n", p=P)[
                    :, :, ds(i * SLAB, SLAB)]).then_inc(lw_in, 16)

            sp.wait_ge(w_used, ph_rkv[2].weight(3, 7))
            lora_second(0)
            with sp.Fori(0, ph_chunk.iters - 1) as i:
                sp.wait_ge(*hd_pe.at("lora", i))
                lora_second(i + 1)
                stream(ph_chunk, i, None, 1, 32)
            stream(ph_chunk, ph_chunk.iters - 1, None, 1, 32)
            out_pieces(ph_rwkv_out, w_o, 4)
            up_pieces(1)
            out_pieces(ph_down[1], w_down[1], DOWN_PIECES)
            for t in range(TT):
                sp.wait_ge(*fin_v.at(f"x{4 * t + 3}"))
                sp.dma_start(out[0].rearrange("(t p) d -> p t d", p=P)[:, t, :], xout[:, t, :]).then_inc(out_done, 16)
            sp.wait_ge(out_done, 16 * TT)

        @block.gpsimd
        def _(pool):
            def sum_squares(n):
                o = outp[n]
                for s in range(NSLAB - 1):
                    pool.wait_ge(*o["a"].at("sq", s))
                    src = sq[:, 2 * s:2 * s + 2, :].rearrange("p t s -> p (t s)")
                    if s == 0:
                        pool.tensor_copy(sqsum[:, :], src).then_inc(*o["g"].inc("add"))
                    else:
                        pool.wait_ge(*o["g"].at("add", s - 1))
                        pool.tensor_tensor(sqsum[:, :], sqsum[:, :], src, ALU.add).then_inc(*o["g"].inc("add"))

            sum_squares(0)
            sum_squares(1)
            def products(i, q):
                t0, g_ = i * 2, hd_g
                if at_start(i, 0):
                    pool.wait_ge(*pr_v.at("pone"))
                else:
                    pool.wait_ge(*pr_pe.at("ln", i - 1))
                if not at_start(i, 0) and not at_start(i - 1, 0):
                    pool.wait_ge(*sc_v.at("yc", i - 2))
                pool.tensor_copy(pcol[:, 0, :], col[:, ds(t0 + C_KK, 2)]).then_inc(*g_.inc("c0"))
                pool.tensor_copy(pcol[:, 1, :], col[:, ds(t0 + C_KA, 2)]).then_inc(*g_.inc("c1"))
                pool.tensor_copy(pcol[:, 2, :], ncol[:, ds(t0, 2)]).then_inc(*g_.inc("c2"))
                pool.tensor_copy(pcol[:, 3, :], col[:, ds(t0 + C_RK, 2)]).then_inc(*g_.inc("c3"))
                pool.tensor_copy(kkr[:, :, :], rk[:, ds(t0, 2), 1, :]).then_inc(*g_.inc("k"))
                pool.wait_ge(*g_.at("k", i))
                waited(pool)
                for p in range(2):
                    pool.tensor_scalar(kkr[:, p, :], kkr[:, p, :], pcol[:, 0, p:p + 1], None,
                                       ALU.mult).then_inc(*g_.inc(f"kk{p}"))
                pool.wait_ge(*g_.at("kk1", i))
                pool.tensor_tensor(sqk[:, :, :], kkr[:, :, :], kkr[:, :, :], ALU.mult).then_inc(*g_.inc("sqk"))
                for p in range(2):
                    pool.wait_ge(*hd_a.at(f"sa{p}", i))
                    waited(pool)
                    pool.tensor_scalar(tmpa[:, p, :], sig[:, 1, p, :], pcol[:, 1, p:p + 1], pcol[:, 2, p:p + 1],
                                       ALU.mult, ALU.add).then_inc(*g_.inc(f"t{p}"))
                pool.wait_ge(*g_.at("t1", i))
                waited(pool)
                pool.tensor_tensor(kp[:, :, :], tmpa[:, :, :], rk[:, ds(t0, 2), 1, :], ALU.mult).then_inc(*g_.inc("kp"))
                pool.wait_ge(*g_.at("kp", i))
                pool.wait_ge(*hd_v.at("p7", i))
                waited(pool)
                pool.tensor_tensor(dec[:, :, :], kp[:, :, :], rk[:, ds(t0, 2), 0, :], ALU.mult).then_inc(*g_.inc("rk"))
                pool.wait_ge(*g_.at("rk", i))
                waited(pool)
                for p in range(2):
                    pool.tensor_scalar(dec[:, p, :], dec[:, p, :], pcol[:, 3, p:p + 1],
                                       None, ALU.mult).then_inc(*g_.inc(f"rk{p}"))
                pool.tensor_copy(vloc[:, :, :], vfm[:, ds(t0, 2), :]).then_inc(*g_.inc("v"))
                pool.tensor_copy(ut[q][:, :, :, :, :].rearrange("p a c u s -> p (a c u) s"),
                                 i64.unsqueeze(1).broadcast_to([P, 2 * CH * 2, HD])).then_inc(*g_.inc("ui"))

            products(0, 0)
            products(1, 1)
            with pool.Fori(1, ph_chunk.iters // 2) as i2:
                products(i2 * 2, 0)
                products(i2 * 2 + 1, 1)
            sum_squares(2)
            sum_squares(3)

        @block.scalar
        def _(sc):
            def hi(ph, i, w):
                k = ph.w_at[w]
                slot, half = ph.raw(k), ph.half(w)
                sc.wait_ge(raw_in[slot], ph.landed(i, k))
                if not at_start(i, ph.w0 + w + 1 - NH):
                    sc.wait_ge(w_used, ph.weight(i, w - NH))
                sc.activation(whi[:, half, :, :].rearrange("p k n -> p (k n)"), slots[slot],
                              ACT.Copy).then_inc(w_hi, 1)

            def hi_new(ph, i, w):
                if not (at_start(i, 0) and w < ph.early):
                    hi(ph, i, w)

            def early(ph, *pieces_):
                for w in pieces_:
                    if ph and w < ph.early:
                        hi(ph, 0, w)

            def laps(n, body):
                body(0, True)
                with sc.Fori(1, n) as i:
                    body(i, False)

            def x_squares(n, x_ready):
                s = norm[n]
                for g in groups:
                    sc.wait_ge(*x_ready(g))
                    sc.activation(sq[:, 4 * g:4 * g + 4, :], x[:, 4 * g:4 * g + 4, :], ACT.Square).then_inc(
                        *s["a"].inc(f"sq{g}"))
                sc.wait_ge(*s["pe"].at("sum"))
                sc.activation(rs[:, :], ps[3][:, 0:S], ACT.Sqrt, bias=eps[0], scale=1.0 / D).then_inc(*s["a"].inc("root"))

            def x_hi(n):
                s = norm[n]
                for g in groups:
                    sc.wait_ge(*s["v"].at(f"t{g}"))
                    src = (vb if g % 2 else tb4)
                    for t in range(4 * g, 4 * g + 4):
                        dst = hb[:, t, 1:S + 1] if n == 2 else xs[:, t, 0, :]
                        last = sc.activation(dst, src[:, t % 4, :], ACT.Identity, bias=shift_col(n, t))
                    last.then_inc(*s["a"].inc(f"hi{g}"))

            def out_proj(n, ph, per_slab, following=None):
                o = outp[n]

                def result(i, s):
                    slab = i * 4 + s
                    sc.wait_ge(w_used, ph.weight(i, (s + 1) * per_slab - 1))
                    src = ps[s][:, :].rearrange("p (m t) -> p m t", m=2)
                    sc.activation(y[:, ds(slab * 2, 2), :], src, ACT.Copy).then_inc(*o["a"].inc("y"))
                    sc.activation(sq[:, ds(slab * 2, 2), :], src, ACT.Square).then_inc(*o["a"].inc("sq"))

                def body(i, first):
                    for s in range(4):
                        for q in range(per_slab):
                            hi_new(ph, i, s * per_slab + q)
                            if s and q == NH - 1:
                                result(i, s - 1)
                    result(i, 3)

                laps(ph.iters, body)
                early(following, 0, 1)
                sc.wait_ge(*o["pe"].at("sum"))
                sc.activation(rs[:, :], ps[4][:, 0:S], ACT.Sqrt, bias=eps[0], scale=1.0 / D).then_inc(
                    *o["root"].inc("root"))
                early(following, 2, 3)

            n_rows = 0

            def crow_in(b, r0, n, src):
                nonlocal n_rows
                sc.dma_start(crow[r0:r0 + n, b, :], src).then_inc(rows_in, 16)
                n_rows += 1

            crow_in(0, 0, KT, rows(a["c"][0]))
            for n, name in enumerate(("rwkv_w0", "rwkv_a0", "rwkv_k_k", "rwkv_k_a")):
                crow_in(0, KT * (n + 1), KT, rows(a[name][0]))
            crow_in(0, KT * 5, KT, a["rwkv_r_k"][0].rearrange("(t h) n -> t (h n)", h=2))
            crow_in(0, KT * 6, KT, rows(a["rwkv_gn_w"][0]))
            crow_in(0, KT * 7, KT, rows(a["rwkv_gn_b"][0]))
            crow_in(1, 0, P, a["norm_g"].rearrange("l j (t p) -> (l j t) p", p=P))
            for n in range(2):
                crow_in(2 + n, 0, MODT, rows(a["mod_b"][n]))
            crow_in(4, 0, 6 * KT, a["rwkv_mu"][0].rearrange("j (t p) -> (j t) p", p=P))
            for n in range(2):
                for tap in range(3):
                    crow_in(5 + 3 * n + tap, 0, 2 * FT, rows(a["ffn_conv_w"][n, tap]))
                crow_in(11 + n, 0, 2 * FT, rows(a["ffn_conv_b"][n]))
            sc.dma_start(xtok[:, :, :], a["x"][0].rearrange("(t p) d -> p t d", p=P)).then_inc(x_in, 16)
            assert n_rows == NROWS, n_rows
            sc.dma_start(wf[:, :, :], fox_w_in[:, :, 3 * D:3 * D + HEADS]).then_inc(fox_in, 16)
            sc.dma_start(bf[:, :], a["fox_b_f"]).then_inc(fox_in, 16)
            sc.dma_start(triu[:, :, :], a["consts"][:, K_TRIU:K_TRIU + TT * S].rearrange(
                "p (t s) -> p t s", t=TT)).then_inc(fox_in, 16)
            sc.dma_start(causal[:, :], a["consts"][:, K_CAUSAL:K_CAUSAL + 3 * P]).then_inc(fox_in, 16)

            sc.wait_ge(*se_v.at("cols"))
            sc.activation(cexp[:, :], col[:, C_COND:C_COND + KT], ACT.Exp, scale=-1.0).then_inc(*se_a.inc("cexp"))

            x_squares(0, lambda g: se_v.at(f"x{2 * g + 1}"))
            early(ph_fox, 0, 1)
            x_hi(0)
            sc.wait_ge(fox_in, 64)
            sc.activation(wfh[:, :, :], wf[:, :, :], ACT.Copy).then_inc(*fg_a.inc("hi"))

            def fox_q(i):
                sc.wait_ge(w_used, ph_fox.weight(i, 3))
                sc.activation(qf[:, :, :], ps[0][:, :].rearrange("p (m t) -> p m t", m=2), ACT.Copy,
                              scale=float(P) ** -0.5).then_inc(*fx_a.inc("q"))

            def fox_k(i):
                sc.wait_ge(w_used, ph_fox.weight(i, 7))
                sc.activation(kf[:, :, :], ps[1][:, :].rearrange("p (m t) -> p m t", m=2),
                              ACT.Copy).then_inc(*fx_a.inc("k"))

            def fox_v(i):
                sc.wait_ge(w_used, ph_fox.weight(i, 11))
                sc.activation(vt_fox[:, :, :], ps[2][:, :].rearrange("p (m t) -> p m t", m=2),
                              ACT.Copy).then_inc(*fx_a.inc("v"))

            def softmax_exp(a_):
                sc.wait_ge(*at_v.at("m11", a_))
                for h in range(2):
                    for t in range(2):
                        lo_, hi_ = (0, P) if t == 0 else (P, 3 * P)
                        sc.activation(ex[:, h, lo_:hi_], sm[:, h, lo_:hi_], ACT.Exp, bias=nmax[:, h, t:t + 1],
                                      accum_out=den[:, h, t:t + 1]).then_inc(*at_a.inc(f"e{h}{t}"))

            def attn_hi(a_):
                sc.wait_ge(*at_pe.at("o", a_))
                for h in range(2):
                    sc.activation(act[:, ds(a_ * 2 + h, 1), 0, :].rearrange("p a s -> p (a s)"), ps[3 + h][:, 0:S],
                                  ACT.Copy).then_inc(*at_a.inc(f"hi{h}"))

            def fox_body(i, first):
                for w in range(12):
                    hi_new(ph_fox, i, w)
                    if w == 2 and not first:
                        softmax_exp(i - 1)
                    if w == 3 and not first:
                        fox_v(i - 1)
                    if w == 7:
                        fox_q(i)
                        if first:
                            sc.wait_ge(*fg_v.at("abs"))
                            sc.activation(gb[:, :, :], ga[:, :, :], ACT.Exp, scale=-1.0).then_inc(*fg_a.inc("e"))
                            sc.wait_ge(*fg_a.at("e"))
                            sc.activation(gb[:, :, :], gb[:, :, :], ACT.Ln, bias=con[:, K_ONE:K_ONE + 1]).then_inc(
                                *fg_a.inc("l"))
                    if w == 10 and not first:
                        attn_hi(i - 1)
                    if w == 11:
                        fox_k(i)

            laps(8, fox_body)
            early(ph_fox_out, 0)
            softmax_exp(7)
            fox_v(7)
            early(ph_fox_out, 1, 2)
            attn_hi(7)
            early(ph_fox_out, 3)
            out_proj(0, ph_fox_out, 4, ph_up[0])

            def up_proj(n):
                ph, s = ph_up[n], up[n]

                def taps(i, half, steps_):
                    sc.wait_ge(w_used, ph.weight(i, 4 * half + 3))
                    src = ps[half][:, :].rearrange("p (m t) -> p m t", m=2)
                    sc.activation(ub[:, 2 * half:2 * half + 2, 2:S + 2], src, ACT.Copy).then_inc(*steps_.inc("u"))
                    for m in range(2):
                        c = i * 2 + (half * FT + m)
                        sc.activation(vb[:, 2 * half + m, :], src[:, m, :], ACT.Identity,
                                      bias=col[:, ds(c + (C_CONVB + 2 * FT * n), 1)],
                                      scale=col[:, ds(c + (C_CONVW + 2 * FT * (3 * n + 2)), 1)]).then_inc(
                                          *steps_.inc(f"t{m}"))

                def gelu(i):
                    sc.wait_ge(*s["v1"].at("c1", i))
                    sc.activation(vb[:, 0:2, :], vb[:, 0:2, :], ACT.Gelu).then_inc(*s["a1"].inc("g"))

                def product_hi(i):
                    sc.wait_ge(*s["v2"].at("prod", i))
                    sc.activation(act[:, ds(i * 2, 2), 0, :], vb[:, 2:4, :], ACT.Copy).then_inc(*s["a2"].inc("hi"))

                def body(i, first):
                    for w in range(8):
                        hi_new(ph, i, w)
                        if w == 1 and not first:
                            gelu(i - 1)
                        if w == 3 and not first:
                            taps(i - 1, 1, s["a2"])
                        if w == 5 and not first:
                            product_hi(i - 1)
                        if w == 7:
                            if first:
                                sc.wait_ge(*s["z"].at("zero"))
                            else:
                                sc.wait_ge(*s["v2"].at("prod", i - 1))
                            taps(i, 0, s["a1"])

                laps(UP_ITERS, body)
                early(ph_down[n], 0)
                gelu(UP_ITERS - 1)
                taps(UP_ITERS - 1, 1, s["a2"])
                early(ph_down[n], 1, 2)
                product_hi(UP_ITERS - 1)
                early(ph_down[n], 3)

            x_squares(1, lambda g: outp[0]["v"].at(f"x{g}"))
            x_hi(1)
            up_proj(0)
            out_proj(1, ph_down[0], DOWN_PIECES, ph_lora)
            x_squares(2, lambda g: outp[1]["v"].at(f"x{g}"))
            x_hi(2)

            def mixed_now(m, g, buf):
                for t in range(2):
                    last = sc.activation(mx[:, buf, t, :], hb[:, ds(g * 2 + t, 1), 1:S + 1].rearrange("p a s -> p (a s)"),
                                         ACT.Copy, scale=omu[:, ds(g * 2 + (KT * MIXES[m] + t), 1)])
                last.then_inc(*mix_now.inc("now"))

            def mixed_hi(m, g, buf):
                sc.wait_ge(*mix_sum.at("sum", g + 8 * m))
                sc.activation(mix_to(m)[:, ds(g * 2, 2), 0, :], mx[:, buf, :, :], ACT.Copy).then_inc(*mix_hi.inc("hi"))

            def mix(m):
                if m >= 2:
                    sc.wait_ge(w_used, mix_free(m))
                for g in range(9):
                    if g < 8:
                        if 8 * m + g >= 4:
                            sc.wait_ge(*mix_lo.at("lo", 8 * m + g - 4))
                        mixed_now(m, g, g % 4)
                    if g:
                        mixed_hi(m, g - 1, (g - 1) % 4)

            sc.wait_ge(*norm[2]["a"].at("hi3"))
            for j, (w0_, nw_, func, dst, src) in enumerate((
                    (0, 2, ACT.Tanh, tw[:, :], ps[4][0:LORA, 0:S]),
                    (2, 2, ACT.Copy, ta[:, :], ps[5][0:LORA, 0:S]),
                    (4, 4, ACT.Sigmoid, tg[:, :, :], ps[6][:, :].rearrange("p (m t) -> p m t", m=2)))):
                mix(j)
                for w in range(w0_, w0_ + nw_):
                    hi_new(ph_lora, 0, w)
                if j:
                    lora_out()
                ready = ph_lora.weight(0, w0_ + nw_ - 1)

                def lora_out(ready=ready, dst=dst, src=src, func=func, name=("tw", "ta", "tg")[j]):
                    sc.wait_ge(w_used, ready)
                    sc.activation(dst, src, func).then_inc(*lo_a.inc(name))
            mix(3)
            lora_out()
            for j in range(3):
                def result(i, s):
                    sc.wait_ge(w_used, ph_rkv[j].weight(i, 4 * s + 3))
                    dst = vfm[:, ds(i * 4 + 2 * s, 2), :] if j == 2 else rk[:, ds(i * 4 + 2 * s, 2), j, :]
                    sc.activation(dst, ps[s][:, :].rearrange("p (m t) -> p m t", m=2),
                                  ACT.Copy).then_inc(*rk_a[j].inc(f"s{s}"))

                def rkv_body(i, first):
                    for w in range(8):
                        hi(ph_rkv[j], i, w)
                        if w == 1 and j < 2:
                            if first:
                                sc.wait_ge(w_used, mix_free(4 + j))
                            sc.wait_ge(*mix_lo.at("lo", i * 2 + (8 * (4 + j) - 1)))
                            for g in range(2):
                                mixed_now(4 + j, i * 2 + g, g)
                        if w == 3 and not first:
                            result(i - 1, 1)
                        if w == 5 and j < 2:
                            for g in range(2):
                                mixed_hi(4 + j, i * 2 + g, g)
                        if w == 7:
                            result(i, 0)

                laps(4, rkv_body)
                result(3, 1)

            def sigmoids(i):
                t0 = i * 2
                sc.wait_ge(*hd_pe.at("lora", i))
                for b, (nm, c0) in enumerate((("sw", C_W0), ("sa", C_A0))):
                    for p in range(2):
                        sc.activation(sig[:, b, p, :], ps[4 + b][:, p * S:p * S + S], ACT.Sigmoid,
                                      bias=col[:, ds(t0 + (c0 + p), 1)]).then_inc(*hd_a.inc(f"{nm}{p}"))
                sc.wait_ge(*hd_a.at("sw1", i))
                sc.activation(dec[:, :, :], sig[:, 0, :, :], ACT.Exp, scale=DECAY_RATE).then_inc(*hd_a.inc("dec"))

            def norms(i, q, again):
                if again:
                    sc.wait_ge(*sc_v.at("o", i - 2))
                sc.activation(flat(gate[q]), ps[6][:, :], ACT.Copy).then_inc(*hd_a.inc("gate"))
                sc.wait_ge(*hd_pe.at("n2", i))
                sc.activation(flat(nrm), ps[4][:, :], ACT.Sqrt).then_inc(*hd_a.inc("nrm"))

            def chunk_head(i, q):
                sc.wait_ge(*pr_v.at("pone"))
                sigmoids(i)
                norms(i, q, False)

            def chunk_lap(i, q, prep=True, turn=True, ahead=True):
                n_ = i - 1

                def out(name, bank):
                    if turn:
                        sc.wait_ge(*sc_pe.at(name, n_))
                        sc.activation((rhs_s if name[0] == "r" else sa)[:, :, :].rearrange("p a s -> p (a s)"),
                                      bank[:, 0:2 * HD], ACT.Copy).then_inc(*sc_a.inc(name))

                def tokens_out(name, dst, b):
                    if prep:
                        sc.wait_ge(*pr_pe.at(f"{name}tok", i))
                        sc.activation(dst[q][:, :, :, :].rearrange("p a c s -> p (a c s)"), ps[b][:, :],
                                      ACT.Copy).then_inc(*pr_a.inc(f"{name}t"))

                def z_out(n):
                    if prep:
                        for p in range(2):
                            sc.wait_ge(*pr_pe.at(f"z{n}p{p}", i))
                            sc.activation(zsb[:, p, :, :].rearrange("p c s -> p (c s)"), ps[p][:, 0:S],
                                          ACT.Copy).then_inc(*pr_a.inc(f"z{n}p{p}"))

                tokens_out("v", vtok, 1)
                out("rhs0", ps[4])
                tokens_out("b", btok, 2)
                out("sa0", ps[5])
                tokens_out("k", ktok, 3)
                for c in range(1, CH):
                    out(f"rhs{c}", ps[4])
                    out(f"sa{c}", ps[5])
                if turn:
                    sc.wait_ge(*sc_pe.at(f"y{CH - 1}", n_))
                    sc.activation(flat(ysb), ps[6][:, :], ACT.Copy).then_inc(*sc_a.inc("y"))
                z_out(1)
                if turn:
                    sc.wait_ge(*sc_v.at("yc", n_))
                    sc.activation(sqy[:, :, :], yc[:, :, :], ACT.Square).then_inc(*sc_a.inc("sqy"))
                    sc.wait_ge(*sc_pe.at("var", n_))
                    sc.activation(flat(nry), ps[5][:, :], ACT.Sqrt, bias=eps[1], scale=1.0 / HD).then_inc(
                        *sc_a.inc("sd"))
                z_out(2)
                if ahead:
                    sigmoids(i + 1)
                z_out(3)
                if ahead:
                    norms(i + 1, 1 - q, turn)
                z_out(4)
                if turn:
                    sc.wait_ge(*sc_v.at("o", n_))
                    sc.activation(act[:, ds(n_ * 2, 2), 0, :], yc[:, :, :], ACT.Copy).then_inc(*sc_a.inc("hi"))
                z_out(5)

            chunk_laps(sc, chunk_head, chunk_lap)
            out_proj(2, ph_rwkv_out, 4, ph_up[1])
            x_squares(3, lambda g: outp[2]["v"].at(f"x{g}"))
            x_hi(3)
            up_proj(1)
            out_proj(3, ph_down[1], DOWN_PIECES)

        @block.vector
        def _(v):
            def lo(ph, i, w):
                k = ph.w_at[w]
                slot, half = ph.raw(k), ph.half(w)
                v.wait_ge(w_hi, ph.weight(i, w))
                v.tensor_tensor(wlo[:, half, :, :].rearrange("p k n -> p (k n)"), slots[slot],
                                whi[:, half, :, :].rearrange("p k n -> p (k n)").bitcast(F32),
                                ALU.subtract).then_inc(raw_done, 1)

            def adaln(ph, i, m):
                k = ph.m_at[m]
                slot, cols = ph.raw(k), unit_cols[ph]
                u, kt = divmod(m, KT)
                v.wait_ge(raw_in[slot], ph.landed(i, k))
                if kt == 0:
                    if ph is ph_mod:
                        v.wait_ge(*se_v.at("cact"))
                    if not at_start(i, ph.raw0 + k):
                        v.wait_ge(raw_done, ph.done(i, k - 1))
                    v.tensor_scalar(macc[:, 0:cols], slots[slot][:, 0:cols], cact[:, 0:1], None,
                                    ALU.mult).then_inc(raw_done, 1)
                    return
                v.wait_ge(raw_done, ph.done(i, ph.m_at[m - 1]))
                if kt == KT - 1 and not at_start(i, ph.unit0 + u):
                    v.wait_ge(mod_summed, ph.unit(i, u - 1))
                v.scalar_tensor_tensor(mfin[:, 0:cols] if kt == KT - 1 else macc[:, 0:cols], slots[slot][:, 0:cols],
                                       cact[:, kt:kt + 1], macc[:, 0:cols], ALU.mult, ALU.add).then_inc(raw_done, 1)

            def adaln_out(ph, i, u=0):
                n = unit_cols[ph] // P
                t = i * (n * ph.units) + (unit_tile0[ph] + u * n)
                v.wait_ge(mod_summed, ph.unit(i, u))
                v.tensor_tensor(mod[:, ds(t, n)], pmod[:, 0:n], col[:, ds(t + C_MODB, n)], ALU.add).then_inc(mod_written, 1)

            def pieces(ph, i, hooks=None):
                w = m = 0
                for c in ph.pattern:
                    if c == "W":
                        if not (at_start(i, 0) and w < ph.early):
                            lo(ph, i, w)
                        if hooks and w in hooks:
                            hooks[w]()
                        w += 1
                    else:
                        adaln(ph, i, m)
                        m += 1

            def early(ph, *pieces_):
                for w in pieces_:
                    if ph and w < ph.early:
                        lo(ph, 0, w)

            def laps(n, body):
                body(0, True)
                with v.Fori(1, n) as i:
                    body(i, False)

            def x_root(n):
                s = norm[n]
                v.wait_ge(*s["a"].at("root"))
                v.reciprocal(rs[:, :], rs[:, :]).then_inc(*s["v"].inc("rinv"))
                v.wait_ge(*s["v"].at("rinv"))

            def x_norm(n):
                s = norm[n]
                layer, which = divmod(n, 2)
                scale = MODT * layer + 3 * KT * which + KT
                v.wait_ge(mod_written, (ph_mod.unit(3), ph_fox.unit(7), ph_down[0].unit(1, 1), ph_chunk.unit(7))[n])
                v.scalar_tensor_tensor(gain_in[:, :], mod[:, scale:scale + KT], 1.0,
                                       col[:, C_NORM + 64 * layer + 32 * which:C_NORM + 64 * layer + 32 * which + KT],
                                       ALU.add, ALU.mult).then_inc(*s["v"].inc("gain"))
                v.wait_ge(*s["v"].at("gain"))
                for g in range(5):
                    if g < 4:
                        buf = vb if g % 2 else tb4
                        if g >= 2 and n == 2:
                            v.wait_ge(*s["a"].at(f"hi{g - 2}"))
                        if g >= 2 and n != 2:
                            v.wait_ge(*s["v"].at(f"lo{g - 2}"))
                        for t in range(4 * g, 4 * g + 4):
                            last = v.scalar_tensor_tensor(buf[:, t % 4, :], x[:, t, :], gain_in[:, t:t + 1], rs[:, :],
                                                          ALU.mult, ALU.mult)
                        last.then_inc(*s["v"].inc(f"t{g}"))
                    if g >= 1 and n != 2:
                        h = g - 1
                        buf = vb if h % 2 else tb4
                        v.wait_ge(*s["a"].at(f"hi{h}"))
                        for t in range(4 * h, 4 * h + 4):
                            last = v.scalar_tensor_tensor(xs[:, t, 1, :], buf[:, t % 4, :], shift_col(n, t),
                                                          xs[:, t, 0, :].bitcast(F32), ALU.add, ALU.subtract)
                        last.then_inc(*s["v"].inc(f"lo{h}"))
                if n == 2:
                    v.wait_ge(*s["a"].at("hi3"))
                    v.wait_ge(*s["v"].at("t3"))
                else:
                    v.wait_ge(*s["v"].at("lo3"))

            def residual(n, following):
                o = outp[n]
                layer, which = divmod(n, 2)
                gt = MODT * layer + 3 * KT * which + 2 * KT
                g0 = C_NORM + 64 * layer + 32 * which + KT
                v.wait_ge(mod_written, (ph_fox.unit(7), ph_fox_out.unit(1), ph_chunk.unit(7), ph_chunk.unit(7))[n])
                v.tensor_tensor(gain_out[:, :], mod[:, gt:gt + KT], col[:, g0:g0 + KT], ALU.mult).then_inc(
                    *o["v"].inc("gain"))
                early(following, 0, 1)
                v.wait_ge(*o["root"].at("root"))
                v.reciprocal(rs[:, :], rs[:, :]).then_inc(*o["v"].inc("rinv"))
                v.wait_ge(*o["v"].at("rinv"))
                for g in groups:
                    for t in range(4 * g, 4 * g + 4):
                        last = v.scalar_tensor_tensor(y[:, t, :], y[:, t, :], gain_out[:, t:t + 1], rs[:, :],
                                                      ALU.mult, ALU.mult)
                    last.then_inc(*o["v"].inc(f"t{g}"))
                    v.wait_ge(*o["v"].at(f"t{g}"))
                    v.tensor_tensor(x[:, 4 * g:4 * g + 4, :], x[:, 4 * g:4 * g + 4, :], y[:, 4 * g:4 * g + 4, :],
                                    ALU.add).then_inc(*o["v"].inc(f"x{g}"))
                v.wait_ge(*o["v"].at("x3"))
                early(following, 2, 3)

            v.wait_ge(*se_pe.at("rows"))
            at_col = 0
            for b, n in enumerate(ROW_COUNTS):
                last = v.tensor_copy(col[:, at_col:at_col + n], ps[b // 4][:, (b % 4) * P:(b % 4) * P + n])
                at_col += n
            assert at_col == C_ALL
            last.then_inc(*se_v.inc("cols"))
            v.wait_ge(*se_v.at("cols"))
            v.tensor_scalar(ncol[:, :], col[:, C_KA:C_KA + KT], -1.0, 1.0, ALU.mult, ALU.add).then_inc(*se_v.inc("ncol"))
            v.tensor_scalar(omu[:, :], col[:, C_MU:C_MU + 6 * KT], -1.0, 1.0, ALU.mult, ALU.add).then_inc(
                *se_v.inc("omu"))
            v.wait_ge(*se_a.at("cexp"))
            v.tensor_scalar(cexp[:, :], cexp[:, :], 1.0, None, ALU.add).then_inc(*se_v.inc("csum"))
            v.wait_ge(*se_v.at("csum"))
            v.reciprocal(cexp[:, :], cexp[:, :]).then_inc(*se_v.inc("ce"))
            v.wait_ge(*se_v.at("ce"))
            v.tensor_tensor(cact[:, :], cexp[:, :], col[:, C_COND:C_COND + KT], ALU.mult).then_inc(*se_v.inc("cact"))
            for g in range(8):
                v.wait_ge(*se_pe.at(f"x{g}"))
                v.tensor_copy(x[:, 2 * g:2 * g + 2, :], ps[4 + g % 3][:, :].rearrange("p (m t) -> p m t", m=2)).then_inc(
                    *se_v.inc(f"x{g}"))

            x_root(0)

            def mod_body(i, first):
                for m in range(KT):
                    adaln(ph_mod, i, m)
                adaln_out(ph_mod, i)

            laps(4, mod_body)
            early(ph_fox, 0, 1)
            x_norm(0)

            v.wait_ge(*fg_a.at("hi"))
            v.tensor_tensor(wfl[:, :, :], wf[:, :, :], wfh[:, :, :].bitcast(F32), ALU.subtract).then_inc(*fg_v.inc("lo"))

            def gate_first():
                v.wait_ge(*fg_pe.at("z"))
                v.tensor_copy(gbf[:, :], ps[3][:, 32:32 + HEADS]).then_inc(*fg_v.inc("b"))
                v.wait_ge(*fg_v.at("b"))
                v.tensor_tensor(gz[:, :, :], ps[3][:, 0:TT * HEADS].rearrange("p (t h) -> p t h", t=TT),
                                gbf[:, :].unsqueeze(1).broadcast_to([P, TT, HEADS]), ALU.add).then_inc(*fg_v.inc("z"))
                v.wait_ge(*fg_v.at("z"))
                v.scalar_tensor_tensor(ga[:, :, :], gz[:, :, :], -1.0, gz[:, :, :], ALU.mult, ALU.max).then_inc(
                    *fg_v.inc("abs"))

            def gate_second():
                v.wait_ge(*fg_a.at("l"))
                v.tensor_scalar(ga[:, :, :], gz[:, :, :], 0.0, None, ALU.min).then_inc(*fg_v.inc("min"))
                v.wait_ge(*fg_v.at("min"))
                v.tensor_tensor(ga[:, :, :], ga[:, :, :], gb[:, :, :], ALU.subtract).then_inc(*fg_v.inc("ls"))

            def select(a_):
                for h in range(2):
                    v.tensor_scalar(nsel[:, h, :], negc[:, :], con[0:HEADS, ds(a_ * 2 + (K_ID + h), 1)], None,
                                    ALU.mult).then_inc(*at_v.inc(f"sel{h}"))

            def softmax_max(a_):
                v.wait_ge(*at_pe.at("s", a_))
                for h in range(2):
                    v.tensor_tensor(sm[:, h, :], ps[3 + h][:, 0:3 * P], causal[:, :], ALU.add).then_inc(
                        *at_v.inc(f"sm{h}"))
                for h in range(2):
                    v.wait_ge(*at_v.at(f"sm{h}", a_))
                    for t in range(2):
                        lo_, hi_ = (0, P) if t == 0 else (P, 3 * P)
                        v.tensor_reduce(nmax[:, h, t:t + 1], sm[:, h, lo_:hi_], AX_X, ALU.max,
                                        negate=True).then_inc(*at_v.inc(f"m{h}{t}"))

            def softmax_den(a_):
                v.wait_ge(*at_a.at("e11", a_))
                v.reciprocal(dinv[:, :, :], den[:, :, :]).then_inc(*at_v.inc("rd"))
                v.wait_ge(*at_v.at("rd", a_))
                for h in range(2):
                    for t in range(2):
                        v.tensor_scalar(diag[:, h, t, :], ident, dinv[:, h, t:t + 1], None,
                                        ALU.mult).then_inc(*at_v.inc(f"d{h}{t}"))

            def probs_out(a_):
                v.wait_ge(*at_pe.at("t", a_))
                for h in range(2):
                    v.tensor_copy(pt[:, h, :], ps[5 + h][:, 0:3 * P]).then_inc(*at_v.inc(f"p{h}"))

            def attn_lo(a_):
                for h in range(2):
                    v.wait_ge(*at_a.at(f"hi{h}", a_))
                    v.tensor_tensor(act[:, ds(a_ * 2 + h, 1), 1, :].rearrange("p a s -> p (a s)"), ps[3 + h][:, 0:S],
                                    act[:, ds(a_ * 2 + h, 1), 0, :].rearrange("p a s -> p (a s)").bitcast(F32),
                                    ALU.subtract).then_inc(*at_v.inc(f"lo{h}"))

            def fox_body(i, first):
                if first:
                    pieces(ph_fox, i, {5: gate_first, 7: gate_second})
                    v.wait_ge(*fg_pe.at("cum"))
                    v.tensor_scalar(negc[:, :], ps[3][0:HEADS, P:P + S], -1.0, None, ALU.mult).then_inc(
                        *fg_v.inc("neg"))
                    v.wait_ge(*fg_v.at("neg"))
                else:
                    pieces(ph_fox, i, {1: lambda: softmax_max(i - 1), 2: lambda: softmax_den(i - 1),
                                       3: lambda: adaln_out(ph_fox, i - 1), 5: lambda: probs_out(i - 1),
                                       9: lambda: attn_lo(i - 1)})
                select(i)

            laps(8, fox_body)
            softmax_max(7)
            early(ph_fox_out, 0)
            softmax_den(7)
            adaln_out(ph_fox, 7)
            early(ph_fox_out, 1)
            probs_out(7)
            early(ph_fox_out, 2)
            attn_lo(7)
            early(ph_fox_out, 3)

            def out_proj(n, ph, following=None):
                def body(i, first):
                    per_slab = ph.nw // 4
                    hooks = {3 * per_slab + 6: lambda: adaln_out(ph, i, 0)} if ph.units == 2 else None
                    pieces(ph, i, hooks)
                    if ph.units:
                        adaln_out(ph, i, ph.units - 1)

                laps(ph.iters, body)
                residual(n, following)

            out_proj(0, ph_fox_out, ph_up[0])

            def up_proj(n):
                ph, s = ph_up[n], up[n]
                v.memset(ub[:, :, 0:2], 0.0).then_inc(*s["z"].inc("zero"))

                def conv(i, half, a_, st_):
                    v.wait_ge(*a_.at("t1", i))
                    for tap, nm in ((1, "p"), (0, "c")):
                        for m in range(2):
                            if tap == 0:
                                v.wait_ge(*st_.at(f"p{m}", i))
                            c = i * 2 + (half * FT + m + C_CONVW + 2 * FT * (3 * n + tap))
                            q = 2 * half + m
                            v.scalar_tensor_tensor(vb[:, q, :], ub[:, q, tap:tap + S], col[:, ds(c, 1)], vb[:, q, :],
                                                   ALU.mult, ALU.add).then_inc(*st_.inc(f"{nm}{m}"))

                def second_half(i):
                    conv(i, 1, s["a2"], s["v2"])
                    v.wait_ge(*s["a1"].at("g", i))
                    v.wait_ge(*s["v2"].at("c1", i))
                    v.tensor_tensor(vb[:, 2:4, :], vb[:, 2:4, :], vb[:, 0:2, :], ALU.mult).then_inc(
                        *s["v2"].inc("prod"))

                def product_lo(i):
                    v.wait_ge(*s["a2"].at("hi", i))
                    v.tensor_tensor(act[:, ds(i * 2, 2), 1, :], vb[:, 2:4, :],
                                    act[:, ds(i * 2, 2), 0, :].bitcast(F32), ALU.subtract).then_inc(*s["v2"].inc("lo"))

                def body(i, first):
                    pieces(ph, i, None if first else {0: lambda: conv(i - 1, 0, s["a1"], s["v1"]),
                                                      4: lambda: second_half(i - 1), 6: lambda: product_lo(i - 1)})

                laps(UP_ITERS, body)
                conv(UP_ITERS - 1, 0, s["a1"], s["v1"])
                early(ph_down[n], 0)
                second_half(UP_ITERS - 1)
                early(ph_down[n], 1)
                product_lo(UP_ITERS - 1)
                early(ph_down[n], 2, 3)
                v.wait_ge(*s["v2"].at("lo", UP_ITERS - 1))

            x_root(1)
            x_norm(1)
            up_proj(0)
            out_proj(1, ph_down[0], ph_lora)
            x_root(2)
            x_norm(2)

            v.memset(hb[:, :, 0:1], 0.0).then_inc(*mix_zero.inc("zero"))
            v.wait_ge(*mix_zero.at("zero"))

            def mixed_sum(m, g, buf):
                v.wait_ge(*mix_now.at("now", g + 8 * m))
                for t in range(2):
                    last = v.scalar_tensor_tensor(
                        mx[:, buf, t, :], hb[:, ds(g * 2 + t, 1), 0:S].rearrange("p a s -> p (a s)"),
                        col[:, ds(g * 2 + (C_MU + KT * MIXES[m] + t), 1)], mx[:, buf, t, :], ALU.mult, ALU.add)
                last.then_inc(*mix_sum.inc("sum"))

            def mixed_lo(m, g, buf):
                v.wait_ge(*mix_hi.at("hi", g + 8 * m))
                v.tensor_tensor(mix_to(m)[:, ds(g * 2, 2), 1, :], mx[:, buf, :, :],
                                mix_to(m)[:, ds(g * 2, 2), 0, :].bitcast(F32), ALU.subtract).then_inc(*mix_lo.inc("lo"))

            def mix(m):
                for g in range(10):
                    if g < 8:
                        mixed_sum(m, g, g % 4)
                    if g >= 2:
                        mixed_lo(m, g - 2, (g - 2) % 4)

            for j, (w0_, nw_) in enumerate(((0, 2), (2, 2), (4, 4))):
                mix(j)
                for w in range(max(w0_, ph_lora.early), w0_ + nw_):
                    lo(ph_lora, 0, w)
            mix(3)
            for j in range(3):
                def rkv_body(i, first):
                    def both(what):
                        for g in range(2):
                            what(4 + j, i * 2 + g, g)

                    pieces(ph_rkv[j], i, {2: lambda: both(mixed_sum), 6: lambda: both(mixed_lo)} if j < 2 else None)

                laps(4, rkv_body)

            v.wait_ge(w_used, ph_rkv[2].weight(3, 7))
            v.wait_ge(*rk_a[2].at("s1", 3))
            v.wait_ge(lvl_in, 16)
            v.memset(zero[:, :], 0.0).then_inc(*pr_v.inc("zero"))
            v.memset(pcum[:, :, :, 0:1], 1.0).then_inc(*pr_v.inc("pone"))
            v.nop().then_inc(*sc_v.inc("first"))

            def decays(i, q):
                c_ = hd_v
                if at_start(i, 0):
                    v.wait_ge(*pr_v.at("pone"))
                v.wait_ge(*hd_a.at("dec", i))
                for n in range(8):
                    p, c = divmod(n, CH)
                    v.tensor_tensor_scan(pcum[:, p, c, 1:HD + 1], dec[:, p, c * HD:c * HD + HD], zero[:, :], 1.0,
                                         ALU.mult, ALU.add).then_inc(*c_.inc(f"p{n}"))
                v.wait_ge(*c_.at("p7", i))
                v.tensor_copy(pend[q][:, :, :], pcum[:, :, :, HD]).then_inc(*c_.inc("pend"))

            def kk_r(i, q):
                c_ = hd_v
                v.wait_ge(*hd_a.at("nrm", i))
                v.tensor_scalar(flat(nrm), flat(nrm), 1e-12, None, ALU.max).then_inc(*c_.inc("nmx"))
                v.wait_ge(*c_.at("nmx", i))
                v.reciprocal(flat(nrm), flat(nrm)).then_inc(*c_.inc("nrc"))
                v.wait_ge(*c_.at("nrc", i))
                v.wait_ge(*hd_g.at("sqk", i))
                v.tensor_tensor(flat(kkr), flat(kkr), flat(nrm), ALU.mult).then_inc(*c_.inc("kkn"))
                v.wait_ge(*c_.at("kkn", i))
                v.tensor_tensor(rr[q][:, :, :, 0, :].rearrange("p a c s -> p (a c) s"), chunks(kkr),
                                pairs(pcum)[:, :, 0:HD], ALU.mult).then_inc(*c_.inc("r0"))

            def decay_r(i, q):
                c_, t0 = hd_v, i * 2
                v.reciprocal(chunks(pinv), pairs(pcum)[:, :, 1:HD + 1]).then_inc(*c_.inc("pinv"))
                for p in range(2):
                    last = v.tensor_tensor(rr[q][:, p, :, 1, :],
                                           rk[:, ds(t0 + p, 1), 0, :].rearrange("p a (c s) -> p (a c) s", s=HD),
                                           pcum[:, p, :, 1:HD + 1], ALU.mult)
                last.then_inc(*c_.inc("r1"))

            def bonus(i, q):
                v.wait_ge(*hd_pe.at("bon", i))
                v.tensor_tensor(bonv[q][:, :, :], ps[5][:, :].rearrange("p (m t) -> p m t", m=2),
                                vfm[:, ds(i * 2, 2), :], ALU.mult).then_inc(*hd_v.inc("bonv"))

            def b_k(i):
                c_ = hd_v
                v.wait_ge(*hd_g.at("t1", i))
                v.wait_ge(*c_.at("r1", i))
                v.tensor_tensor(bneg[:, :, :], kkr[:, :, :], sig[:, 1, :, :], ALU.mult).then_inc(*c_.inc("kka"))
                v.wait_ge(*c_.at("kka", i))
                v.scalar_tensor_tensor(flat(bneg), flat(bneg), -1.0, flat(pinv), ALU.mult, ALU.mult).then_inc(
                    *c_.inc("bneg"))
                v.wait_ge(*c_.at("bneg", i))
                v.wait_ge(*hd_g.at("kp", i))
                v.tensor_tensor(flat(khat), flat(kp), flat(pinv), ALU.mult).then_inc(*c_.inc("khat"))

            def chunk_head(i, q):
                decays(i, q)
                kk_r(i, q)
                decay_r(i, q)
                bonus(i, q)

            def chunk_lap(i, q, prep=True, turn=True, ahead=True):
                n_, w = i - 1, 1 - q
                m_ = [0]

                def some(n):
                    for _ in range(n if prep else 0):
                        adaln(ph_chunk, i, m_[0])
                        m_[0] += 1

                def decayed(c):
                    if not turn:
                        return
                    if c == 0:
                        v.memset(st[:, 0, :, :], 0.0).then_inc(*sc_v.inc("z"))
                        v.wait_ge(*sc_v.at("z", n_))
                    else:
                        v.wait_ge(*sc_v.at(f"st{c - 1}b", n_))
                    for p in range(2):
                        v.tensor_scalar(std[:, p, :], st[:, c % 2, p, :], pend[w][:, p, c:c + 1], None,
                                        ALU.mult).then_inc(*sc_v.inc(f"sp{c}" + "ab"[p]))

                def state(c):
                    if not turn:
                        return
                    v.wait_ge(*sc_v.at(f"sp{c}b", n_))
                    v.wait_ge(*sc_pe.at(f"m{c}", n_))
                    for p in range(2):
                        v.scalar_tensor_tensor(st[:, (c + 1) % 2, p, :], ps[4][:, P + p * HD:P + p * HD + HD],
                                               pend[w][:, p, c:c + 1], std[:, p, :], ALU.mult, ALU.add).then_inc(
                                                   *sc_v.inc(f"st{c}" + "ab"[p]))

                def masked(p):
                    if not prep:
                        return
                    bank = ps[p][:, :].rearrange("p (c u s) -> p c u s", c=CH, u=2)
                    v.wait_ge(*pr_pe.at(f"pb{p}", i))
                    if p == 0:
                        v.wait_ge(*hd_g.at("ui", i))
                    waited(v)
                    v.copy_predicated(ut[q][:, p, :, 0, :], level(0, 0, CH), bank[:, :, 0, :]).then_inc(
                        *pr_v.inc(f"ub{p}"))
                    v.tensor_tensor(arb[q][:, p, :, :], bank[:, :, 1, :], mask(K_MBK + HD, CH), ALU.mult).then_inc(
                        *pr_v.inc(f"arb{p}"))
                    v.wait_ge(*pr_pe.at(f"pk{p}", i))
                    v.tensor_tensor(lka[q][:, p, :, :, :].rearrange("p c u s -> p c (u s)"),
                                    ps[2 + p][:, :].rearrange("p (c s) -> p c s", c=CH),
                                    con[:, K_MBK:K_MBK + P].unsqueeze(1).broadcast_to([P, CH, P]),
                                    ALU.mult).then_inc(*pr_v.inc(f"lk{p}"))

                def doubled(n, p):
                    if not prep:
                        return
                    v.wait_ge(*pr_pe.at(f"u{n}p{p}", i))
                    waited(v)
                    if n == LEVELS - 1:
                        v.copy_predicated(ut[q][:, p, :, 0, :], level(n, 0, CH),
                                          ps[2 + p][:, :].rearrange("p (c u s) -> p c u s", c=CH, u=2)[:, :, 0, :]
                                          ).then_inc(*pr_v.inc(f"u{n}p{p}"))
                    else:
                        v.copy_predicated(
                            ut[q][:, p, :, :, :].rearrange("p c u s -> p c (u s)"),
                            lvl[:, n, :].bitcast(I32).unsqueeze(1).broadcast_to([P, CH, P]),
                            ps[2 + p][:, :].rearrange("p (c s) -> p c s", c=CH)).then_inc(*pr_v.inc(f"u{n}p{p}"))

                decayed(0)
                if prep:
                    b_k(i)
                some(2)
                state(0)
                decayed(1)
                some(2)
                masked(0)
                state(1)
                decayed(2)
                some(2)
                masked(1)
                state(2)
                decayed(3)
                some(2)
                if prep:
                    v.wait_ge(*pr_pe.at("ln", i))
                    both = ps[0][:, :].rearrange("p (c s) -> p c s", s=HD)
                    v.tensor_tensor(lnm[:, :, :, :].rearrange("p a c s -> p (a c) s"), both, mask(K_ML, 2 * CH),
                                    ALU.mult).then_inc(*pr_v.inc("ln"))
                    v.copy_predicated(ut[q][:, :, :, 1, :].rearrange("p a c s -> p (a c) s"), level(0, 1, 2 * CH),
                                      both).then_inc(*pr_v.inc("tb"))
                state(3)
                some(2)
                if turn:
                    v.wait_ge(*sc_pe.at("mean", n_))
                    v.scalar_tensor_tensor(flat(yc), ps[4][:, :], -1.0 / HD, flat(ysb), ALU.mult, ALU.add).then_inc(
                        *sc_v.inc("yc"))
                some(1)
                doubled(1, 0)
                some(1)
                doubled(1, 1)
                if turn:
                    v.wait_ge(*sc_a.at("sd", n_))
                    v.reciprocal(flat(nry), flat(nry)).then_inc(*sc_v.inc("rs"))
                    v.wait_ge(*sc_v.at("rs", n_))
                    v.tensor_tensor(flat(yc), flat(yc), flat(nry), ALU.mult).then_inc(*sc_v.inc("yn"))
                doubled(2, 0)
                if turn:
                    v.wait_ge(*sc_v.at("yn", n_))
                    for p in range(2):
                        v.tensor_scalar(yc[:, p, :], yc[:, p, :], col[:, ds(n_ * 2 + (C_GNW + p), 1)],
                                        col[:, ds(n_ * 2 + (C_GNB + p), 1)], ALU.mult, ALU.add).then_inc(
                                            *sc_v.inc(f"gn{p}"))
                doubled(2, 1)
                if turn:
                    v.wait_ge(*sc_v.at("gn1", n_))
                    v.tensor_tensor(flat(yc), flat(yc), flat(bonv[w]), ALU.add).then_inc(*sc_v.inc("bo"))
                    v.wait_ge(*sc_v.at("bo", n_))
                    v.tensor_tensor(flat(yc), flat(yc), flat(gate[w]), ALU.mult).then_inc(*sc_v.inc("o"))
                some(KT - 2 - m_[0])
                if ahead:
                    decays(i + 1, w)
                doubled(3, 0)
                some(1)
                doubled(3, 1)
                if ahead:
                    kk_r(i + 1, w)
                doubled(4, 0)
                some(1)
                doubled(4, 1)
                if ahead:
                    decay_r(i + 1, w)
                if turn:
                    v.wait_ge(*sc_a.at("hi", n_))
                    v.tensor_tensor(act[:, ds(n_ * 2, 2), 1, :], yc[:, :, :],
                                    act[:, ds(n_ * 2, 2), 0, :].bitcast(F32), ALU.subtract).then_inc(*sc_v.inc("lo"))
                if ahead:
                    bonus(i + 1, w)
                doubled(5, 0)
                doubled(5, 1)
                assert not prep or m_[0] == KT
                if prep:
                    adaln_out(ph_chunk, i)

            chunk_laps(v, chunk_head, chunk_lap)
            out_proj(2, ph_rwkv_out, ph_up[1])
            x_root(3)
            x_norm(3)
            up_proj(1)
            out_proj(3, ph_down[1])
            for n in range(8):
                v.wait_ge(*fin_pe.at(f"x{n}"))
                v.tensor_copy(xout[:, n // 4, (n % 4) * 512:(n % 4) * 512 + 512], ps[n % 4][:, :]).then_inc(
                    *fin_v.inc(f"x{n}"))

        @block.tensor
        def _(pe):
            def slab(ph, i, w0_, n, bank, src, tokens=False, ready=None, only=None):
                for q in range(n) if only is None else only:
                    w = w0_ + q
                    half = ph.half(w)
                    pe.wait_ge(raw_done, ph.done(i, ph.w_at[w]))
                    if ready and ready(q):
                        pe.wait_ge(*ready(q))
                    for k in range(PIECE_KT):
                        kt = PIECE_KT * q + k
                        begin, end = q == 0 and k == 0, q == n - 1 and k == PIECE_KT - 1
                        for m in range(2):
                            for h, (w_, s_) in enumerate(((whi, 0), (whi, 1), (wlo, 0))):
                                if tokens:
                                    lhs, rhs = src[:, kt, s_, m * P:m * P + P], w_[:, half, k, :]
                                else:
                                    lhs, rhs = w_[:, half, k, m * P:m * P + P], src[:, kt, s_, :]
                                last = pe.matmul(ps[bank][:, m * S:m * S + S], lhs, rhs,
                                                 start=begin and m == 0 and h == 0, stop=end and h == 2,
                                                 skip_group_check=True)
                    last.then_inc(w_used, 1)

            def adaln_sum(ph, i, u=0):
                pe.wait_ge(raw_done, ph.done(i, ph.m_at[u * KT + KT - 1]))
                if not at_start(i, ph.unit0 + u):
                    pe.wait_ge(mod_written, ph.unit(i, u - 1))
                n = unit_cols[ph] // P
                for t in range(n):
                    last = pe.matmul(pmod[:, t:t + 1], mfin[:, t * P:t * P + P], ones[:, 0:1], start=True, stop=True,
                                     skip_group_check=True)
                last.then_inc(mod_summed, 1)

            def x_sum(n):
                s = norm[n]
                for t in range(KT):
                    if t % 4 == 0:
                        pe.wait_ge(*s["a"].at(f"sq{t // 4}"))
                    last = pe.matmul(ps[3][:, 0:S], ones, sq[:, t, :], start=t == 0, stop=t == KT - 1)
                last.then_inc(*s["pe"].inc("sum"))

            def out_proj(n, ph, per_slab, ready, started=False):
                o = outp[n]
                def body(i):
                    for s in range(4):
                        if s == 0 and started and at_start(i, 0):
                            continue
                        slab(ph, i, s * per_slab, per_slab, s, act,
                             ready=(lambda q: ready if q == per_slab - 1 else None) if s == 0 else None)
                        if ph.units == 2 and s == 2:
                            adaln_sum(ph, i, 0)
                    if ph.units:
                        adaln_sum(ph, i, ph.units - 1)

                if started:
                    body(0)
                with pe.Fori(1 if started else 0, ph.iters) as i:
                    body(i)
                pe.wait_ge(*o["g"].at("add", NSLAB - 2))
                for m in range(2):
                    pe.matmul(ps[4][:, 0:S], ones, sqsum[:, m * S:m * S + S], start=m == 0, stop=False)
                pe.wait_ge(*o["a"].at("sq", NSLAB - 1))
                for m in range(2):
                    last = pe.matmul(ps[4][:, 0:S], ones, sq[:, KT - 2 + m, :], start=False, stop=m == 1)
                last.then_inc(*o["pe"].inc("sum"))

            pe.wait_ge(const_in, 16)
            pe.wait_ge(rows_in, 16 * (NROWS))
            for b, n in enumerate(ROW_COUNTS):
                last = pe.transpose(ps[b // 4][:, (b % 4) * P:(b % 4) * P + n], crow[0:n, b, :], ident[0:n, 0:n])
            last.then_inc(*se_pe.inc("rows"))
            pe.wait_ge(x_in, 16)
            for g in range(8):
                if g >= 3:
                    pe.wait_ge(*se_v.at(f"x{g - 3}"))
                for m in range(2):
                    for t in range(TT):
                        last = pe.transpose(ps[4 + g % 3][:, m * S + t * P:m * S + t * P + P],
                                            xtok[:, t, (2 * g + m) * P:(2 * g + m) * P + P], ident)
                last.then_inc(*se_pe.inc(f"x{g}"))
            x_sum(0)
            adaln_sum(ph_mod, 0)
            with pe.Fori(1, 4) as i:
                adaln_sum(ph_mod, i)

            def scores(a_):
                pe.wait_ge(*fx_a.at("k", a_))
                pe.wait_ge(*at_v.at("sel1", a_))
                for h in range(2):
                    for t in range(2):
                        dst = ps[3 + h][:, 0:P] if t == 0 else ps[3 + h][:, P:3 * P]
                        n = P * (t + 1)
                        pe.matmul(dst, qf[:, h, t * P:t * P + P], kf[:, h, 0:n], start=True, stop=False,
                                  skip_group_check=True)
                        last = pe.matmul(dst, ones[0:HEADS, :], nsel[:, h, 0:n], start=False, stop=True,
                                         skip_group_check=True)
                last.then_inc(*at_pe.inc("s"))

            def probs(a_):
                pe.wait_ge(*at_v.at("d11", a_))
                for h in range(2):
                    for b in range(3):
                        last = pe.matmul(ps[5 + h][:, b * P:b * P + P], ex[:, h, b * P:b * P + P],
                                         diag[:, h, min(b, 1), :], start=True, stop=True, skip_group_check=True)
                last.then_inc(*at_pe.inc("t"))

            def values(a_):
                pe.wait_ge(*at_v.at("p1", a_))
                pe.wait_ge(*fx_a.at("v", a_))
                for h in range(2):
                    pe.matmul(ps[3 + h][:, 0:S], vt_fox[:, 0, h * P:h * P + P], pt[:, h, 0:S], start=True, stop=False,
                              skip_group_check=True)
                    last = pe.matmul(ps[3 + h][:, P:S], vt_fox[:, 1, h * P:h * P + P], pt[:, h, S:3 * P],
                                     start=False, stop=True, skip_group_check=True)
                last.then_inc(*at_pe.inc("o"))

            def gate_logits():
                pe.wait_ge(*norm[0]["v"].at("lo3"))
                pe.wait_ge(*fg_v.at("lo"))
                for t in range(TT):
                    for kt in range(KT):
                        for h, (s_, w_) in enumerate(((0, wfh), (1, wfh), (0, wfl))):
                            pe.matmul(ps[3][:, t * HEADS:t * HEADS + HEADS], xs[:, kt, s_, t * P:t * P + P],
                                      w_[:, kt, :], start=kt == 0 and h == 0, stop=kt == KT - 1 and h == 2,
                                      skip_group_check=True)
                pe.matmul(ps[3][:, 32:32 + HEADS], ones[0:1, :], bf[0:1, :], start=True, stop=True,
                          skip_group_check=True).then_inc(*fg_pe.inc("z"))

            def gate_sums():
                pe.wait_ge(*fg_v.at("ls"))
                for t in range(TT):
                    last = pe.matmul(ps[3][0:HEADS, P:P + S], ga[:, t, :], triu[:, t, :], start=t == 0, stop=t == 1,
                                     skip_group_check=True)
                last.then_inc(*fg_pe.inc("cum"))

            def ready0(q):
                return norm[0]["v"].at(f"lo{q}")

            pe.wait_ge(fox_in, 64)
            slab(ph_fox, 0, 0, 4, 0, xs, ready=ready0)
            gate_logits()
            slab(ph_fox, 0, 4, 4, 1, xs)
            slab(ph_fox, 0, 8, 4, 2, xs, tokens=True)
            gate_sums()
            adaln_sum(ph_fox, 0)
            with pe.Fori(1, 8) as i:
                scores(i - 1)
                slab(ph_fox, i, 0, 4, 0, xs)
                probs(i - 1)
                slab(ph_fox, i, 4, 4, 1, xs)
                values(i - 1)
                slab(ph_fox, i, 8, 4, 2, xs, tokens=True)
                adaln_sum(ph_fox, i)
            scores(7)
            slab(ph_fox_out, 0, 0, 4, 0, act, only=(0,))
            probs(7)
            slab(ph_fox_out, 0, 0, 4, 0, act, only=(1,))
            values(7)
            slab(ph_fox_out, 0, 0, 4, 0, act, only=(2, 3), ready=lambda q: at_v.at("lo1", 7) if q == 3 else None)
            out_proj(0, ph_fox_out, 4, None, started=True)
            x_sum(1)

            def up_proj(n):
                with pe.Fori(0, UP_ITERS) as i:
                    slab(ph_up[n], i, 0, 4, 0, xs, ready=lambda q: norm[2 * n + 1]["v"].at(f"lo{q}"))
                    slab(ph_up[n], i, 4, 4, 1, xs)

            up_proj(0)
            out_proj(1, ph_down[0], DOWN_PIECES, up[0]["v2"].at("lo", UP_ITERS - 1))
            x_sum(2)

            for j, (w0_, nw_) in enumerate(((0, 2), (2, 2))):
                for q in range(nw_):
                    w = w0_ + q
                    pe.wait_ge(raw_done, ph_lora.done(0, w))
                    pe.wait_ge(*mix_lo.at("lo", 8 * j + 4 * q + 3))
                    for k in range(8):
                        kt = 8 * q + k
                        for h, (w_, s_) in enumerate(((whi, 0), (whi, 1), (wlo, 0))):
                            wk = w_[:, ph_lora.half(w), :, :].rearrange("p k n -> p (k n)")[:, k * LORA:(k + 1) * LORA]
                            last = pe.matmul(ps[4 + j][0:LORA, 0:S], wk, mix_to(j)[:, kt, s_, :], start=kt == 0 and h == 0,
                                             stop=kt == KT - 1 and h == 2)
                    last.then_inc(w_used, 1)
            slab(ph_lora, 0, 4, 4, 6, mix_to(2), ready=lambda q: mix_lo.at("lo", 8 * 2 + 2 * q + 1))
            for j in range(3):
                with pe.Fori(0, 4) as i:
                    slab(ph_rkv[j], i, 0, 4, 0, mix_to(3 + j), ready=lambda q: mix_lo.at("lo", 8 * (3 + j) + 2 * q + 1))
                    slab(ph_rkv[j], i, 4, 4, 1, mix_to(3 + j))

            pe.wait_ge(*lo_a.at("tg"))

            def small_mm(dst, lhs, rhs, start=True, stop=True):
                return pe.matmul(dst, lhs, rhs, start=start, stop=stop, skip_group_check=True)

            def loras(i, again):
                pe.wait_ge(lw_in, i * 48 + 48)
                if again:
                    pe.wait_ge(*sc_v.at("yc", i - 2))
                    pe.wait_ge(*sc_a.at("sd", i - 2))
                for p in range(2):
                    small_mm(ps[4][:, p * S:p * S + S], lw[0:LORA, 0, p * P:p * P + P], tw[:, :])
                    small_mm(ps[5][:, p * S:p * S + S], lw[0:LORA, 1, p * P:p * P + P], ta[:, :])
                    for k in range(2):
                        last = small_mm(ps[6][:, p * S:p * S + S], lw[:, 2 + k, p * P:p * P + P], tg[:, k, :],
                                        k == 0, k == 1)
                last.then_inc(*hd_pe.inc("lora"))

            def wide(bank, src, name):
                for p in range(2):
                    last = small_mm(bank[:, p * S:p * S + S], blk, src[:, p, :])
                last.then_inc(*name)

            def kk_norms(i):
                pe.wait_ge(*hd_a.at("sw1", i))
                pe.wait_ge(*hd_g.at("sqk", i))
                wide(ps[4], sqk, hd_pe.inc("n2"))

            def bonuses(i):
                pe.wait_ge(*hd_g.at("rk1", i))
                wide(ps[5], dec, hd_pe.inc("bon"))

            def chunk_head(i, q):
                pe.wait_ge(*pr_v.at("pone"))
                loras(i, False)
                kk_norms(i)
                bonuses(i)

            def chunk_lap(i, q, prep=True, turn=True, ahead=True):
                c_, n_, w = pr_pe, i - 1, 1 - q

                def turned(name, bank, src, *ready):
                    for r_ in ready:
                        pe.wait_ge(*r_)
                    waited(pe)
                    for p in range(2):
                        for c in range(CH):
                            for h in heads:
                                last_ = small_mm(bank[h, (p * CH + c) * HD:(p * CH + c + 1) * HD],
                                                 src[h, p, c * HD:(c + 1) * HD], i64[h, :])
                    last_.then_inc(*c_.inc(name))

                def by_kk_r(name, bank, src, p, *ready):
                    for r_ in ready:
                        pe.wait_ge(*r_)
                    waited(pe)
                    for c in range(CH):
                        for h in heads:
                            last_ = small_mm(bank[h, c * P:c * P + P], src[h, p, c * HD:(c + 1) * HD],
                                             rr[q][h, p, c, :, :].rearrange("p u s -> p (u s)"))
                    last_.then_inc(*c_.inc(name))

                def rhs(c):
                    if not turn:
                        return
                    if c:
                        pe.wait_ge(*sc_v.at(f"st{c - 1}b", n_))
                    else:
                        pe.wait_ge(*sc_v.at("z", n_))
                    waited(pe)
                    for p in range(2):
                        for h in heads:
                            small_mm(ps[4][h, p * HD:p * HD + HD], rr[w][h, p, c, 0, :], st[h, c % 2, p, :], True, False)
                            last_ = small_mm(ps[4][h, p * HD:p * HD + HD], lka[w][h, p, c, 0, :], vtok[w][h, p, c, :],
                                             False, True)
                    last_.then_inc(*sc_pe.inc(f"rhs{c}"))

                def solve(c):
                    if not turn:
                        return
                    pe.wait_ge(*sc_a.at(f"rhs{c}", n_))
                    waited(pe)
                    for p in range(2):
                        for h in heads:
                            last_ = small_mm(ps[5][h, p * HD:p * HD + HD], ut[w][h, p, c, 0, :], rhs_s[h, p, :])
                    last_.then_inc(*sc_pe.inc(f"sa{c}"))

                def state_y(c):
                    if not turn:
                        return
                    pe.wait_ge(*sc_a.at(f"sa{c}", n_))
                    waited(pe)
                    for p in range(2):
                        for h in heads:
                            dst = ps[4][h, P + p * HD:P + p * HD + HD]
                            small_mm(dst, btok[w][h, p, c, :], sa[h, p, :], True, False)
                            last_ = small_mm(dst, ktok[w][h, p, c, :], vtok[w][h, p, c, :], False, True)
                    last_.then_inc(*sc_pe.inc(f"m{c}"))
                    for p in range(2):
                        for h in heads:
                            dst = ps[6][h, (p * CH + c) * HD:(p * CH + c + 1) * HD]
                            small_mm(dst, st[h, c % 2, p, :], rr[w][h, p, c, 1, :], True, False)
                            small_mm(dst, vtok[w][h, p, c, :], lka[w][h, p, c, 1, :], False, False)
                            last_ = small_mm(dst, sa[h, p, :], arb[w][h, p, c, :], False, True)
                    last_.then_inc(*sc_pe.inc(f"y{c}"))

                def z_mm(n):
                    if not prep:
                        return
                    for p in range(2):
                        pe.wait_ge(*(pr_v.at("tb", i) if n == 1 else pr_v.at(f"u{n - 1}p{p}", i)))
                        waited(pe)
                        for c in range(CH):
                            for h in heads:
                                last_ = small_mm(ps[p][h, c * HD:(c + 1) * HD], lnm[h, p, c, :],
                                                 ut[q][h, p, c, 0, :])
                        last_.then_inc(*c_.inc(f"z{n}p{p}"))

                def u_mm(n):
                    if not prep:
                        return
                    for p in range(2):
                        pe.wait_ge(*pr_a.at(f"z{n}p{p}", i))
                        waited(pe)
                        for c in range(CH):
                            for h in heads:
                                last_ = small_mm(ps[2 + p][h, c * P:c * P + HD], ut[q][h, p, c, 1, :], zsb[h, p, c, :])
                                if n < LEVELS - 1:
                                    last_ = small_mm(ps[2 + p][h, c * P + HD:(c + 1) * P], zsb[h, p, c, :],
                                                     ut[q][h, p, c, 1, :])
                        last_.then_inc(*c_.inc(f"u{n}p{p}"))

                if prep:
                    pe.wait_ge(*pr_v.ended(i))
                    pe.wait_ge(*hd_v.at("bonv", i))
                    turned("vtok", ps[1], vloc, hd_g.at("v", i))
                else:
                    pe.wait_ge(*pr_v.ended(i))
                    pe.wait_ge(*sc_v.ended(n_))
                rhs(0)
                if prep:
                    turned("btok", ps[2], bneg, hd_v.at("bneg", i))
                solve(0)
                if prep:
                    turned("ktok", ps[3], khat, hd_v.at("khat", i))
                state_y(0)
                rhs(1)
                if prep:
                    by_kk_r("pb0", ps[0], bneg, 0)
                solve(1)
                if prep:
                    by_kk_r("pk0", ps[2], khat, 0, pr_a.at("bt", i))
                state_y(1)
                rhs(2)
                if prep:
                    by_kk_r("pb1", ps[1], bneg, 1, pr_a.at("vt", i))
                solve(2)
                if prep:
                    by_kk_r("pk1", ps[3], khat, 1, pr_a.at("kt", i))
                state_y(2)
                rhs(3)
                if prep:
                    pe.wait_ge(*pr_v.at("arb0", i))
                    waited(pe)
                    for p in range(2):
                        for c in range(CH):
                            for h in heads:
                                last = small_mm(ps[0][h, (p * CH + c) * HD:(p * CH + c + 1) * HD],
                                                rr[q][h, p, c, 0, :], bneg[h, p, c * HD:(c + 1) * HD])
                    last.then_inc(*c_.inc("ln"))
                solve(3)
                state_y(3)
                z_mm(1)
                if turn:
                    pe.wait_ge(*sc_v.at(f"st{CH - 1}b", n_))
                    pe.wait_ge(*sc_a.at("y", n_))
                    wide(ps[4], ysb, sc_pe.inc("mean"))
                u_mm(1)
                if turn:
                    pe.wait_ge(*sc_a.at("sqy", n_))
                    wide(ps[5], sqy, sc_pe.inc("var"))
                z_mm(2)
                if ahead:
                    loras(i + 1, turn)
                u_mm(2)
                z_mm(3)
                u_mm(3)
                if ahead:
                    kk_norms(i + 1)
                z_mm(4)
                u_mm(4)
                if ahead:
                    bonuses(i + 1)
                z_mm(5)
                if prep:
                    adaln_sum(ph_chunk, i)
                u_mm(5)

            chunk_laps(pe, chunk_head, chunk_lap)
            out_proj(2, ph_rwkv_out, 4, sc_v.ended(8))
            x_sum(3)
            up_proj(1)
            out_proj(3, ph_down[1], DOWN_PIECES, up[1]["v2"].at("lo", UP_ITERS - 1))
            for n in range(8):
                pe.wait_ge(*outp[3]["v"].at(f"x{n % 4}"))
                if n >= 4:
                    pe.wait_ge(*fin_v.at(f"x{n - 4}"))
                for q in range(4):
                    t = 4 * (n % 4) + q
                    last = pe.transpose(ps[n % 4][:, q * P:q * P + P], x[:, t, (n // 4) * P:(n // 4) * P + P], ident)
                last.then_inc(*fin_pe.inc(f"x{n}"))


_INS = ["x", "c", "mod_w", "mod_b", "norm_g", "fox_w_in", "fox_b_f", "fox_w_out", "rwkv_mu", "rwkv_w0", "rwkv_w1",
        "rwkv_w2", "rwkv_a0", "rwkv_a1", "rwkv_a2", "rwkv_g1", "rwkv_g2", "rwkv_k_k", "rwkv_k_a", "rwkv_r_k",
        "rwkv_w_r", "rwkv_w_k", "rwkv_w_v", "rwkv_w_o", "rwkv_gn_w", "rwkv_gn_b", "ffn_w_in", "ffn_conv_w",
        "ffn_conv_b", "ffn_w_out"]


def kernel(**inputs):
    import concourse.bacc as _bacc
    from concourse.bass_utils import run_bass_kernel_spmd as _run

    nc = _bacc.Bacc("TRN2", target_bir_lowering=False, num_devices=1)
    arrays, aps = {}, {}
    for name in _INS + ["consts"]:
        array = shape_constants() if name == "consts" else np.ascontiguousarray(inputs[name])
        arrays[f"in_{name}"] = array
        aps[name] = nc.dram_tensor(f"in_{name}", array.shape, F32, kind="ExternalInput").ap()
    out = nc.dram_tensor("out", (1, S, D), F32, kind="ExternalOutput").ap()
    trunk(nc, aps, out)
    r = _run(nc, [arrays], core_ids=[0])
    return r.results[0]["out"]
```
